# Optimizing a Trainium2 kernel written in Bass

```python
import math
import jax, jax.numpy as jnp
from jax import lax
import numpy as np

D_MODEL = 1024
BATCH = 1
SEQ = 256
DEPTH = 4

N_MIXERS = 3
BLOCK = 128
N_BUCKETS = 32
MAX_DISTANCE = 128
N_BIAS_CH = 16
DA_HEADS = 8
DA_QK_DIM = 64
DA_V_DIM = 2 * DA_QK_DIM
SB_HEADS = 16
SB_DIM = D_MODEL // SB_HEADS
SW_Q_HEADS = 16
SW_KV_HEADS = 4
SW_DIM = 64
SW_WINDOW = 128
D_FF = 2752
CONV_W = 3
EPS = 1e-6
NEG = -1e30
N_A = (DEPTH + 2) // 3
N_B = (DEPTH + 1) // 3
N_C = DEPTH // 3


def rmsnorm(x, g):
    xf = x.astype(jnp.float32)
    y = xf * lax.rsqrt(jnp.mean(xf * xf, axis=-1, keepdims=True) + EPS)
    return (y * g.astype(jnp.float32)).astype(x.dtype)

def t5_bucket(dist):
    max_exact = N_BUCKETS // 2
    d = jnp.maximum(dist, 0)
    large = max_exact + (jnp.log(jnp.maximum(d, 1).astype(jnp.float32) / max_exact)
                         / math.log(MAX_DISTANCE / max_exact) * (N_BUCKETS - max_exact)).astype(jnp.int32)
    large = jnp.minimum(large, N_BUCKETS - 1)
    return jnp.where(d < max_exact, d, large)

def lambda_init_fn(layer):
    return 0.8 - 0.6 * math.exp(-0.3 * layer)

def diff_attention(h, w_qkv, lam, subln, rel_bias, lambda_init):
    B, S, _ = h.shape
    nb = S // BLOCK
    qk_w = DA_HEADS * 2 * DA_QK_DIM
    qkv = h @ w_qkv
    q, k, v = jnp.split(qkv, [qk_w, 2 * qk_w], axis=-1)
    q = q.reshape(B, S, DA_HEADS, 2, DA_QK_DIM)
    k = k.reshape(B, S, DA_HEADS, 2, DA_QK_DIM)
    v = v.reshape(B, S, DA_HEADS, DA_V_DIM)
    lf = lam.astype(jnp.float32)
    lam_full = jnp.exp(jnp.sum(lf[0] * lf[1])) - jnp.exp(jnp.sum(lf[2] * lf[3])) + lambda_init
    bias_tab = rel_bias.astype(jnp.float32).reshape(N_BUCKETS, DA_HEADS, 2)
    k_pos = jnp.arange(S)
    scale = DA_QK_DIM ** -0.5
    q_blocks = jnp.moveaxis(q.reshape(B, nb, BLOCK, DA_HEADS, 2, DA_QK_DIM), 1, 0)

    def block(args):
        qb, start = args
        q_pos = start + jnp.arange(BLOCK)
        dist = q_pos[:, None] - k_pos[None, :]
        bias = jnp.transpose(bias_tab[t5_bucket(dist)], (2, 3, 0, 1))
        s = jnp.einsum('bqhjd,bkhjd->bhjqk', qb, k).astype(jnp.float32) * scale + bias
        s = jnp.where(dist >= 0, s, NEG)
        p = jax.nn.softmax(s, axis=-1)
        a = p[:, :, 0] - lam_full * p[:, :, 1]
        return jnp.einsum('bhqk,bkhe->bqhe', a.astype(v.dtype), v)

    o = lax.map(block, (q_blocks, jnp.arange(nb) * BLOCK))
    o = jnp.moveaxis(o, 0, 1).reshape(B, S, DA_HEADS, DA_V_DIM)
    o = rmsnorm(o, subln) * (1.0 - lambda_init)
    return o.reshape(B, S, DA_HEADS * DA_V_DIM)

def stick_breaking_attention(h, w_qkv):
    B, S, _ = h.shape
    nb = S // BLOCK
    qkv = h @ w_qkv
    q, k, v = jnp.split(qkv, 3, axis=-1)
    q = q.reshape(B, S, SB_HEADS, SB_DIM)
    k = k.reshape(B, S, SB_HEADS, SB_DIM)
    v = v.reshape(B, S, SB_HEADS, SB_DIM)
    k_pos = jnp.arange(S)
    scale = SB_DIM ** -0.5
    q_blocks = jnp.moveaxis(q.reshape(B, nb, BLOCK, SB_HEADS, SB_DIM), 1, 0)

    def block(args):
        qb, start = args
        q_pos = start + jnp.arange(BLOCK)
        strict = k_pos[None, :] < q_pos[:, None]
        z = jnp.einsum('bqhd,bkhd->bhqk', qb, k).astype(jnp.float32) * scale
        log_1m_beta = jnp.where(strict, jax.nn.log_sigmoid(-z), 0.0)
        between = lax.cumsum(log_1m_beta, axis=3, reverse=True) - log_1m_beta
        a = jnp.where(strict, jnp.exp(jax.nn.log_sigmoid(z) + between), 0.0)
        return jnp.einsum('bhqk,bkhd->bqhd', a.astype(v.dtype), v)

    o = lax.map(block, (q_blocks, jnp.arange(nb) * BLOCK))
    return jnp.moveaxis(o, 0, 1).reshape(B, S, SB_HEADS * SB_DIM)

def sliding_window_attention(h, w_qkv, sinks, rel_bias):
    B, S, _ = h.shape
    nb = S // BLOCK
    G = SW_Q_HEADS // SW_KV_HEADS
    q_w = SW_Q_HEADS * SW_DIM
    kv_w = SW_KV_HEADS * SW_DIM
    qkv = h @ w_qkv
    q, k, v = jnp.split(qkv, [q_w, q_w + kv_w], axis=-1)
    q = q.reshape(B, nb, BLOCK, SW_KV_HEADS, G, SW_DIM)
    k = k.reshape(B, nb, BLOCK, SW_KV_HEADS, SW_DIM)
    v = v.reshape(B, nb, BLOCK, SW_KV_HEADS, SW_DIM)

    def band(t):
        prev = jnp.pad(t[:, :-1], ((0, 0), (1, 0), (0, 0), (0, 0), (0, 0)))
        return jnp.concatenate([prev, t], axis=2)

    kb, vb = band(k), band(v)
    i = jnp.arange(BLOCK)[:, None]
    j = jnp.arange(2 * BLOCK)[None, :]
    dist = i + BLOCK - j
    in_window = (dist >= 0) & (dist < SW_WINDOW)
    blk = jnp.arange(nb)[:, None, None]
    valid = in_window[None] & ((blk * BLOCK - BLOCK + j[None]) >= 0)
    bias = rel_bias.astype(jnp.float32)[t5_bucket(dist)]
    bias = bias.reshape(BLOCK, 2 * BLOCK, SW_KV_HEADS, G).transpose(2, 3, 0, 1)
    s = jnp.einsum('bnqgrd,bnkgd->bngrqk', q, kb).astype(jnp.float32) * (SW_DIM ** -0.5) + bias
    s = jnp.where(valid[None, :, None, None], s, NEG)
    sink = jnp.broadcast_to(sinks.astype(jnp.float32).reshape(SW_KV_HEADS, G, 1, 1), s.shape[:-1] + (1,))
    p = jax.nn.softmax(jnp.concatenate([s, sink], axis=-1), axis=-1)[..., :-1]
    o = jnp.einsum('bngrqk,bnkgd->bnqgrd', p.astype(vb.dtype), vb)
    return o.reshape(B, S, q_w)

def conv_gated_ffn(h, w_up, conv_w, conv_b, w_down):
    u = h @ w_up
    C = u.shape[-1]
    u = lax.conv_general_dilated(u, conv_w[:, None, :].astype(u.dtype), window_strides=(1,),
                                 padding=[(CONV_W - 1, 0)], dimension_numbers=('NWC', 'WIO', 'NWC'),
                                 feature_group_count=C) + conv_b
    gate, val = jnp.split(u, 2, axis=-1)
    return (jax.nn.silu(gate) * val) @ w_down

def first_inputs(seed: int = 0) -> dict:
    key = jax.random.key(seed)
    ks = jax.random.split(key, 20)
    D, F = D_MODEL, D_FF
    nrm = lambda k, shape, fan_in: jax.random.normal(k, shape, jnp.float32) * fan_in ** -0.5
    gain = lambda k, shape: 1.0 + 0.05 * jax.random.normal(k, shape, jnp.float32)
    return {
        'x': jax.random.normal(ks[0], (BATCH, SEQ, D), jnp.float32),
        'rel_bias': 0.5 * jax.random.normal(ks[1], (N_BUCKETS, N_BIAS_CH), jnp.float32),
        'attn_norm': gain(ks[2], (DEPTH, D)),
        'ffn_norm': gain(ks[3], (DEPTH, D)),
        'w_o': nrm(ks[4], (DEPTH, D, D), D),
        'da_w_qkv': nrm(ks[5], (N_A, D, 2 * DA_HEADS * 2 * DA_QK_DIM + DA_HEADS * DA_V_DIM), D),
        'da_lambda': 0.1 * jax.random.normal(ks[6], (N_A, 4, DA_QK_DIM), jnp.float32),
        'da_subln': gain(ks[7], (N_A, DA_V_DIM)),
        'sb_w_qkv': nrm(ks[8], (N_B, D, 3 * SB_HEADS * SB_DIM), D),
        'sw_w_qkv': nrm(ks[9], (N_C, D, (SW_Q_HEADS + 2 * SW_KV_HEADS) * SW_DIM), D),
        'sw_sinks': 0.5 * jax.random.normal(ks[10], (N_C, SW_Q_HEADS), jnp.float32),
        'ffn_w_up': nrm(ks[11], (DEPTH, D, 2 * F), D),
        'ffn_conv_w': nrm(ks[12], (DEPTH, CONV_W, 2 * F), CONV_W),
        'ffn_conv_b': 0.02 * jax.random.normal(ks[13], (DEPTH, 2 * F), jnp.float32),
        'ffn_w_down': nrm(ks[14], (DEPTH, F, D), F),
        'final_norm': gain(ks[15], (D,)),
    }

def first_block(x, rel_bias, attn_norm, ffn_norm, w_o, da_w_qkv, da_lambda, da_subln, sb_w_qkv,
              sw_w_qkv, sw_sinks, ffn_w_up, ffn_conv_w, ffn_conv_b, ffn_w_down, final_norm):
    for layer in range(DEPTH):
        mixer = layer % N_MIXERS
        slot = layer // N_MIXERS
        h = rmsnorm(x, attn_norm[layer])
        if mixer == 0:
            m = diff_attention(h, da_w_qkv[slot], da_lambda[slot], da_subln[slot], rel_bias,
                               lambda_init_fn(layer))
        elif mixer == 1:
            m = stick_breaking_attention(h, sb_w_qkv[slot])
        else:
            m = sliding_window_attention(h, sw_w_qkv[slot], sw_sinks[slot], rel_bias)
        x = x + m @ w_o[layer]
        h = rmsnorm(x, ffn_norm[layer])
        x = x + conv_gated_ffn(h, ffn_w_up[layer], ffn_conv_w[layer], ffn_conv_b[layer], ffn_w_down[layer])
    return rmsnorm(x, final_norm)


DEPTH_2 = 1

PLE_DIM = 256
D_POOL = 512
POOL_WINDOWS = (2, 4, 8, 16)
N_POOL_GROUPS = len(POOL_WINDOWS)
POOL_GROUP = D_POOL // N_POOL_GROUPS
D_ATTN = D_MODEL - D_POOL
N_HEADS = 8
HEAD_DIM = D_ATTN // N_HEADS
MOBA_BLOCK = 256
MOBA_TOPK = 3
Q_CHUNK = 32
NUM_BUCKETS = 32
D_FF_2 = 2816
CONV_WIDTH = 3
D_IN = D_POOL + 3 * D_ATTN


def rms_norm(x, g):
    xf = x.astype(jnp.float32)
    y = xf * lax.rsqrt(jnp.mean(xf * xf, axis=-1, keepdims=True) + EPS)
    return (y * g.astype(jnp.float32)).astype(x.dtype)

def pool_mixer(u, w_pool, pool_scale):
    B, S, _ = u.shape
    uf = u.astype(jnp.float32)
    cpad = jnp.pad(jnp.cumsum(uf, axis=1), ((0, 0), (1, 0), (0, 0)))
    pos = jnp.arange(S)
    outs = []
    for g, w in enumerate(POOL_WINDOWS):
        c_g = cpad[:, :, g * POOL_GROUP:(g + 1) * POOL_GROUP]
        lagged = jnp.pad(c_g[:, :S + 1 - w], ((0, 0), (w - 1, 0), (0, 0)))
        count = jnp.minimum(pos + 1, w).astype(jnp.float32)[None, :, None]
        mean = (c_g[:, 1:] - lagged) / count
        outs.append(mean - uf[:, :, g * POOL_GROUP:(g + 1) * POOL_GROUP])
    pooled = jnp.stack(outs, axis=2)
    mixed = jnp.einsum('bsgc,gcd->bsgd', pooled, w_pool.astype(jnp.float32))
    return (mixed.reshape(B, S, D_POOL) * pool_scale.astype(jnp.float32)).astype(u.dtype)

def rel_bucket(dist):
    n = jnp.maximum(dist, 0)
    max_exact = NUM_BUCKETS // 2
    nf = jnp.maximum(n, 1).astype(jnp.float32)
    large = max_exact + (jnp.log(nf / max_exact) / math.log(MAX_DISTANCE / max_exact)
                         * (NUM_BUCKETS - max_exact)).astype(jnp.int32)
    large = jnp.minimum(large, NUM_BUCKETS - 1)
    return jnp.where(n < max_exact, n, large)

def moba_attention(q, k, v, rel_bias):
    B, S = q.shape[0], q.shape[1]
    nb = -(-S // MOBA_BLOCK)
    s_pad = nb * MOBA_BLOCK
    pad = ((0, 0), (0, s_pad - S), (0, 0), (0, 0))
    q, k, v = [jnp.pad(t, pad).transpose(0, 2, 1, 3) for t in (q, k, v)]
    k_blk = k.reshape(B, N_HEADS, nb, MOBA_BLOCK, HEAD_DIM)
    v_blk = v.reshape(B, N_HEADS, nb, MOBA_BLOCK, HEAD_DIM)
    k_mean = jnp.mean(k_blk.astype(jnp.float32), axis=3)
    gate = jnp.einsum('bhsd,bhnd->bhsn', q.astype(jnp.float32), k_mean)
    q_blk_idx = jnp.arange(s_pad) // MOBA_BLOCK
    past = jnp.arange(nb)[None, :] < q_blk_idx[:, None]
    gate = jnp.where(past, gate, -jnp.inf)
    n_sel = min(MOBA_TOPK, nb)
    _, sel = lax.top_k(gate, n_sel)
    sel_valid = sel < q_blk_idx[:, None]

    scale = HEAD_DIM ** -0.5
    bias_t = rel_bias.astype(jnp.float32).T
    b_idx = jnp.arange(B)[:, None, None, None]
    h_idx = jnp.arange(N_HEADS)[None, :, None, None]
    key_off = jnp.arange(MOBA_BLOCK)
    n_sel_keys = n_sel * MOBA_BLOCK

    def chunk(ci):
        start = ci * Q_CHUNK
        qc = lax.dynamic_slice_in_dim(q, start, Q_CHUNK, axis=2)
        sc = lax.dynamic_slice_in_dim(sel, start, Q_CHUNK, axis=2)
        vc = lax.dynamic_slice_in_dim(sel_valid, start, Q_CHUNK, axis=2)
        t = start + jnp.arange(Q_CHUNK)
        j = start // MOBA_BLOCK
        k_sel = k_blk[b_idx, h_idx, sc]
        v_sel = v_blk[b_idx, h_idx, sc]
        key_pos = sc[..., None] * MOBA_BLOCK + key_off
        bias_sel = bias_t[h_idx[..., None], rel_bucket(t[:, None, None] - key_pos)]
        l_sel = jnp.einsum('bhqd,bhqnkd->bhqnk', qc, k_sel).astype(jnp.float32) * scale + bias_sel
        l_sel = jnp.where(vc[..., None], l_sel, -jnp.inf)
        k_own = lax.dynamic_index_in_dim(k_blk, j, axis=2, keepdims=False)
        v_own = lax.dynamic_index_in_dim(v_blk, j, axis=2, keepdims=False)
        d_own = t[:, None] - (j * MOBA_BLOCK + key_off)[None, :]
        bias_own = bias_t[:, rel_bucket(d_own)]
        l_own = jnp.einsum('bhqd,bhkd->bhqk', qc, k_own).astype(jnp.float32) * scale + bias_own
        l_own = jnp.where(d_own >= 0, l_own, -jnp.inf)
        logits = jnp.concatenate([l_sel.reshape(B, N_HEADS, Q_CHUNK, n_sel_keys), l_own], axis=-1)
        probs = jax.nn.softmax(logits, axis=-1).astype(v.dtype)
        p_sel = probs[..., :n_sel_keys].reshape(B, N_HEADS, Q_CHUNK, n_sel, MOBA_BLOCK)
        p_own = probs[..., n_sel_keys:]
        return (jnp.einsum('bhqnk,bhqnkd->bhqd', p_sel, v_sel)
                + jnp.einsum('bhqk,bhkd->bhqd', p_own, v_own))

    outs = lax.map(chunk, jnp.arange(s_pad // Q_CHUNK))
    out = outs.transpose(1, 0, 3, 2, 4).reshape(B, s_pad, N_HEADS, HEAD_DIM)[:, :S]
    return out.reshape(B, S, D_ATTN)

def conv_ffn(h, w_up, conv_w, conv_b, w_down):
    S = h.shape[1]
    gate, val = jnp.split(h @ w_up, 2, axis=-1)
    gp = jnp.pad(gate, ((0, 0), (CONV_WIDTH - 1, 0), (0, 0)))
    conv = conv_b + gp[:, 0:S] * conv_w[0]
    for kk in range(1, CONV_WIDTH):
        conv = conv + gp[:, kk:kk + S] * conv_w[kk]
    return (jax.nn.gelu(conv, approximate=True) * val) @ w_down

def second_inputs(seed: int = 0) -> dict:
    key = jax.random.key(seed)
    ks = jax.random.split(key, 20)
    f32 = jnp.float32
    nrm = lambda k, shape, s: jax.random.normal(k, shape, f32) * s
    gain = lambda k: 1.0 + nrm(k, (DEPTH_2, D_MODEL), 0.05)
    return {
        "x": nrm(ks[0], (BATCH, SEQ, D_MODEL), 1.0),
        "p": nrm(ks[1], (DEPTH_2, BATCH, SEQ, PLE_DIM), 1.0),
        "rel_bias": nrm(ks[2], (NUM_BUCKETS, N_HEADS), 0.5),
        "g_mix_pre": gain(ks[3]),
        "g_mix_post": gain(ks[4]),
        "g_ffn_pre": gain(ks[5]),
        "g_ffn_post": gain(ks[6]),
        "w_in": nrm(ks[7], (DEPTH_2, D_MODEL, D_IN), D_MODEL ** -0.5),
        "w_pool": nrm(ks[8], (DEPTH_2, N_POOL_GROUPS, POOL_GROUP, POOL_GROUP), POOL_GROUP ** -0.5),
        "pool_scale": 1.0 + nrm(ks[9], (DEPTH_2, D_POOL), 0.1),
        "w_out": nrm(ks[10], (DEPTH_2, D_MODEL, D_MODEL), D_MODEL ** -0.5),
        "w_up": nrm(ks[11], (DEPTH_2, D_MODEL, 2 * D_FF_2), D_MODEL ** -0.5),
        "conv_w": nrm(ks[12], (DEPTH_2, CONV_WIDTH, D_FF_2), CONV_WIDTH ** -0.5),
        "conv_b": nrm(ks[13], (DEPTH_2, D_FF_2), 0.02),
        "w_down": nrm(ks[14], (DEPTH_2, D_FF_2, D_MODEL), D_FF_2 ** -0.5),
        "w_ple": nrm(ks[15], (DEPTH_2, PLE_DIM, D_MODEL), PLE_DIM ** -0.5),
        "w_ple_gate": nrm(ks[16], (DEPTH_2, D_MODEL, D_MODEL), D_MODEL ** -0.5),
    }

def second_block(x, p, rel_bias, g_mix_pre, g_mix_post, g_ffn_pre, g_ffn_post, w_in, w_pool,
              pool_scale, w_out, w_up, conv_w, conv_b, w_down, w_ple, w_ple_gate):
    B, S, _ = x.shape
    for i in range(DEPTH_2):
        h = rms_norm(x, g_mix_pre[i])
        proj = h @ w_in[i]
        u, q, k, v = jnp.split(proj, [D_POOL, D_POOL + D_ATTN, D_POOL + 2 * D_ATTN], axis=-1)
        y_pool = pool_mixer(u, w_pool[i], pool_scale[i])
        y_attn = moba_attention(q.reshape(B, S, N_HEADS, HEAD_DIM),
                                k.reshape(B, S, N_HEADS, HEAD_DIM),
                                v.reshape(B, S, N_HEADS, HEAD_DIM), rel_bias)
        y = jnp.concatenate([y_pool, y_attn], axis=-1) @ w_out[i]
        x = x + rms_norm(y, g_mix_post[i])
        h = rms_norm(x, g_ffn_pre[i])
        x = x + rms_norm(conv_ffn(h, w_up[i], conv_w[i], conv_b[i], w_down[i]), g_ffn_post[i])
        x = x + (p[i] @ w_ple[i]) * jax.nn.sigmoid(x @ w_ple_gate[i])
    return x


def setup_inputs(seed=0):
    out = dict(first_inputs(seed))
    for name, value in second_inputs(seed + 1).items():
        if name != "x":
            out[name + "_2"] = value
    return out


def reference(
    x, rel_bias, attn_norm, ffn_norm, w_o, da_w_qkv, da_lambda, da_subln, sb_w_qkv, sw_w_qkv,
    sw_sinks, ffn_w_up, ffn_conv_w, ffn_conv_b, ffn_w_down, final_norm, p_2, rel_bias_2,
    g_mix_pre_2, g_mix_post_2, g_ffn_pre_2, g_ffn_post_2, w_in_2, w_pool_2, pool_scale_2,
    w_out_2, w_up_2, conv_w_2, conv_b_2, w_down_2, w_ple_2, w_ple_gate_2,
):
    x = first_block(
        x, rel_bias, attn_norm, ffn_norm, w_o, da_w_qkv, da_lambda, da_subln, sb_w_qkv,
        sw_w_qkv, sw_sinks, ffn_w_up, ffn_conv_w, ffn_conv_b, ffn_w_down, final_norm,
    )
    return second_block(
        x, p_2, rel_bias_2, g_mix_pre_2, g_mix_post_2, g_ffn_pre_2, g_ffn_post_2, w_in_2,
        w_pool_2, pool_scale_2, w_out_2, w_up_2, conv_w_2, conv_b_2, w_down_2, w_ple_2,
        w_ple_gate_2,
    )


_drawn_inputs = setup_inputs


def setup_inputs(seed=0):
    import zlib

    import numpy as np

    out = dict(_drawn_inputs(seed))
    spreads = {}
    factors = {'sw_sinks': 4.085, 'conv_b_2': 5.066}
    for name, (base, spread) in spreads.items():
        noise = np.random.default_rng([zlib.crc32(name.encode()), seed]).standard_normal(out[name].shape)
        drawn = base * np.exp(spread * noise) if base else spread * noise
        out[name] = __import__('jax').numpy.asarray(drawn.astype(out[name].dtype))
    for name, factor in factors.items():
        out[name] = (out[name] * factor).astype(out[name].dtype)
    return out
```

```python
from contextlib import ExitStack

import numpy as np

import concourse.bass as bass
import concourse.mybir as mybir
from concourse.alu_op_type import AluOpType as ALU

F32 = mybir.dt.float32
F32R = mybir.dt.float32r
ACT = mybir.ActivationFunctionType

P = 128
S = 256
QB = 128
D = 1024
DT = D // P
FT = 22
RING = 3
STD = DT * 2 * P
DOWN = FT * P
GATE = STD + 2 * 2 * P
NEG = -1e30
EPS = 1e-6
CAUSAL = QB + S
NVEC = 383

PARAM = {}
_n = 0
for _name, _width in (("attn_norm", 4 * DT), ("ffn_norm", 4 * DT), ("final_norm", DT),
                      ("mix_pre", DT), ("mix_post", DT), ("ffn_pre", DT), ("ffn_post", DT),
                      ("conv", 4 * FT * 8), ("conv2", FT * 4), ("subln", 2), ("sinks", 8 * 4),
                      ("pool_scale", 4), ("inv_count", 4 * 16)):
    PARAM[_name] = _n
    _n += _width
NPAR = _n

STAGES = []
SIZES = []
for _kind, _count, _width in (
        ("da", 12, STD), ("wo", 4, STD), ("up", FT, STD), ("down", DT, DOWN),
        ("sb", 12, STD), ("wo", 4, STD), ("up", FT, STD), ("down", DT, DOWN),
        ("sw", 6, STD), ("wo", 4, STD), ("up", FT, STD), ("down", DT, DOWN),
        ("da", 12, STD), ("wo", 4, STD), ("up", FT, STD), ("down", DT, DOWN),
        ("mix", 9, STD), ("wo", 4, STD), ("up", FT, STD), ("down", DT, DOWN),
        ("gate", 4, GATE)):
    STAGES.append((_kind, len(SIZES), _count))
    SIZES += [_width] * _count
CHUNKS = len(SIZES)
EXP_AND_LN = 6
WINDOWS = (2, 4, 8, 16)
POOL_STEPS = sum(w.bit_length() - 1 + 4 for w in WINDOWS)


def lambda_init(layer):
    return 0.8 - 0.6 * float(np.exp(-0.3 * layer))


def build(nc, xT, w_std, w_down, w_gate, params, consts, lam, onehot, tables, pT, out):
    ctx = ExitStack()
    with ctx:
        def sb(name, shape, dt=F32):
            return ctx.enter_context(nc.sbuf_tensor(name, shape, dt))

        def sem(name):
            return ctx.enter_context(nc.semaphore(name))

        w_raw = sb("w_raw", [P, RING, DOWN])
        w_hi = sb("w_hi", [P, RING, DOWN], F32R)
        w_lo = sb("w_lo", [P, RING, DOWN], F32R)
        x = sb("x", [P, DT, S])
        h_hi = sb("h_hi", [P, DT, S], F32R)
        h_lo = sb("h_lo", [P, DT, S], F32R)
        act_hi = sb("act_hi", [P, FT, S], F32R)
        act_lo = sb("act_lo", [P, FT, S], F32R)
        par = sb("par", [P, NPAR])
        cst = sb("cst", [P, 4 * P])
        ident, ones = cst[:, 0:P], cst[:, P:2 * P]
        neg_tri, neg_ones = cst[:, 2 * P:3 * P], cst[:, 3 * P:4 * P]
        proj = sb("proj", [P, 5, S])
        vtok = sb("vtok", [P, 2, S])
        tmp = sb("tmp", [P, 12, S])
        sq = sb("sq", [P, 2, 2 * S])
        acc = sb("acc", [P, 2 * S])
        rstd = sb("rstd", [P, S])
        small = sb("small", [P, 2, 5, 4])
        odd = sb("odd", [P, 8])
        wait_mark = sb("wait_mark", [P, 2])
        u_sb = sb("u_sb", [P, 4, S])

        prob = tmp[:, 0:6, :].rearrange("p a b -> p (a b)").rearrange("p (h m c) -> p h m c", h=2, m=2)
        probT = tmp[:, 6:12, :].rearrange("p a b -> p (a b)").rearrange("p (h m c) -> p h m c", h=2, m=2)
        cgate, cval = tmp[:, 0:3, :], tmp[:, 3:6, :]

        banks = [ctx.enter_context(nc.psum_tensor(f"bank{b}", [P, 2 * S], F32)) for b in range(8)]
        pj = banks[0:3]
        val_bank = banks[3:6]
        sc = banks[3:5]
        tp = banks[5:7]
        ov = banks[7]

        arrived = [sem(f"arrived{s}") for s in range(RING)]
        hi_ready = sem("hi_ready")
        lo_ready = sem("lo_ready")
        used = sem("used")
        bank_free = sem("bank_free")
        setup_in = sem("setup_in")
        x_in = sem("x_in")
        credits = sem("credits")
        chain_a = sem("chain_a")
        sq_ready = sem("sq_ready")
        acc_done = sem("acc_done")
        x_ready = sem("x_ready")
        stat_done = sem("stat_done")
        rstd_done = sem("rstd_done")
        hf_done = sem("hf_done")
        h_hi_done = sem("h_hi_done")
        h_lo_even = sem("h_lo_even")
        h_lo_odd = sem("h_lo_odd")
        conv_init = sem("conv_init")
        conv_part = sem("conv_part")
        gated = sem("gated")
        prod_done = sem("prod_done")
        act_hi_done = sem("act_hi_done")
        act_free = sem("act_free")
        bias_in = [sem(f"bias_in{b}") for b in range(2)]
        scores_done = sem("scores_done")
        scores_taken = sem("scores_taken")
        dve_step = sem("dve_step")
        nmax_ready = sem("nmax_ready")
        sink_shift = sem("sink_shift")
        exp_done = sem("exp_done")
        probs_done = sem("probs_done")
        trans_done = sem("trans_done")
        probT_done = sem("probT_done")
        pv_done = sem("pv_done")
        head_out = sem("head_out")
        head_sq = sem("head_sq")
        head_stat = sem("head_stat")
        head_rstd = sem("head_rstd")
        head_norm = sem("head_norm")
        mix_hi = sem("mix_hi")
        mix_lo = sem("mix_lo")
        log_done = sem("log_done")
        sp_done = sem("sp_done")
        sp_masked = sem("sp_masked")
        cum_done = sem("cum_done")
        a_exp = sem("a_exp")
        a_masked = sem("a_masked")
        pooled = sem("pooled")
        vec_psum = sem("vec_psum")
        vec_sb = sem("vec_sb")
        vec_out = sem("vec_out")
        tab_in = sem("tab_in")
        p_in = sem("p_in")
        p_hi = sem("p_hi")
        p_lo = sem("p_lo")
        sig_done = sem("sig_done")
        emb_done = sem("emb_done")
        out_ready = sem("out_ready")
        stored = sem("stored")

        vec_dram = nc.dram_tensor("vec_dram", (3, 16, NVEC), F32, kind="Internal")

        def param(name, k=0, width=1):
            at = PARAM[name] + k
            return par[:, bass.ds(at, width)] if not isinstance(at, int) else par[:, at:at + width]

        def slot_of(c0, k):
            return (c0 + k) % RING

        NORMS = []
        SUM_UNITS = {}
        total = 0
        for name, n in ([("x", 4)] + [(f"{k}{l}", n) for l in range(4) for k, n in (("wo", 4), ("down", 8))]
                        + [("final", 4), ("wo4", 4), ("res_a", 4), ("down4", 8)]):
            SUM_UNITS[name] = (total, n, len(NORMS))
            NORMS.append(name)
            total += n

        block = ctx.enter_context(nc.Block())

        @block.sync
        def _(sp):
            sp.dma_start(par[:, :], params).then_inc(setup_in, 16)
            sp.dma_start(cst[:, :], consts).then_inc(setup_in, 16)
            sp.dma_start(x[:, :, :], xT).then_inc(x_in, 16)
            source = {STD: w_std, DOWN: w_down, GATE: w_gate}
            seen = {STD: 0, DOWN: 0, GATE: 0}

            def load(c, slot, width, row, wait=True):
                if wait:
                    sp.wait_ge(lo_ready, c - RING + 1)
                sp.dma_start(w_raw[:, slot, 0:width], source[width][row]).then_inc(arrived[slot], 16)

            c = 0
            while c < CHUNKS:
                width = SIZES[c]
                n = 1
                while c + n < CHUNKS and SIZES[c + n] == width:
                    n += 1
                row = seen[width]
                k = 0
                if c == 0:
                    for k in range(RING):
                        load(k, k, width, k, wait=False)
                    k = RING
                turns = (n - k) // RING
                if turns > 1:
                    with sp.Fori(0, turns) as i:
                        for j in range(RING):
                            load(i * RING + (c + k + j), slot_of(c, k + j), width, i * RING + (row + k + j))
                    k += turns * RING
                while k < n:
                    load(c + k, slot_of(c, k), width, row + k)
                    k += 1
                seen[width] += n
                c += n
            for k in range(4):
                sp.wait_ge(out_ready, k + 1)
                sp.dma_start(out[:, 2 * k:2 * k + 2, :], x[:, 2 * k:2 * k + 2, :]).then_inc(stored, 16)
            sp.wait_ge(stored, 64)

        @block.scalar
        def _(act):
            def split_hi(c, slot, width, turn):
                act.wait_ge(arrived[slot], turn * 16 + 16)
                act.copy(w_hi[:, slot, 0:width], w_raw[:, slot, 0:width]).then_inc(hi_ready, 1)

            def next_split(c0, k, i=None):
                n = c0 + k + RING
                if i is None and n >= CHUNKS:
                    return
                shift = 0 if i is None else i * RING
                act.wait_ge(used, shift + (c0 + k + 1))
                turn = n // RING if i is None else i + n // RING
                split_hi(shift + n, n % RING, SIZES[n], turn)

            def squares(unit, source, width, parity):
                act.wait_ge(acc_done, unit + 1)
                act.activation(sq[:, parity, 0:width], source, ACT.Square).then_inc(sq_ready, 1)

            chained = [0]

            def chain(ins):
                chained[0] += 1
                ins.then_inc(chain_a, 1)
                act.wait_ge(chain_a, chained[0])

            def rms(norm):
                act.wait_ge(stat_done, norm + 1)
                chain(act.activation(rstd[:, :], ov[:, 0:S], ACT.Ln, bias=odd[:, 7:8], scale=1.0 / D))
                act.activation(rstd[:, :], rstd[:, :], ACT.Exp, scale=-0.5).then_inc(rstd_done, 1)

            def split_h(app):
                for k in range(DT):
                    act.wait_ge(hf_done, app * DT + k + 1)
                    act.copy(h_hi[:, k, :], tmp[:, k, :]).then_inc(h_hi_done, 1)

            def load_tables(functions):
                act.add_instruction(mybir.InstLoadActFuncSet(name=nc.get_next_instruction_name(),
                                                             act_func_set_id=functions))

            def exps(s_half, slot, sink):
                act.wait_ge(nmax_ready, s_half + 1)
                if sink:
                    act.wait_ge(sink_shift, sink)
                    act.activation(small[:, slot, 4, :], small[:, slot, 4, :], ACT.Exp)
                for m in range(2):
                    for qb, (a, b) in enumerate(((0, QB), (QB, CAUSAL))):
                        n = 2 * m + qb
                        last = act.activation(prob[:, slot, m, a:b], prob[:, slot, m, a:b], ACT.Exp,
                                              bias=small[:, slot, 1, n:n + 1],
                                              accum_out=small[:, slot, 2, n:n + 1])
                last.then_inc(exp_done, 1)

            def copy_probT(s_half, slot, maps):
                act.wait_ge(trans_done, s_half + 1)
                for m in range(maps):
                    last = act.copy(probT[:, slot, m, :], tp[m][:, 0:CAUSAL])
                last.then_inc(probT_done, 1)

            def mix_high(half, tile):
                act.wait_ge(pv_done, half + 1)
                act.copy(act_hi[:, tile, :], ov[:, 0:S]).then_inc(mix_hi, 1)

            def head_squares(half, d_half, slot):
                act.wait_ge(pv_done, half + 1)
                act.copy(u_sb[:, slot, :], ov[:, 0:S]).then_inc(head_out, 1)
                act.wait_ge(head_out, d_half + 1)
                act.activation(u_sb[:, 2 + slot, :], u_sb[:, slot, :], ACT.Square).then_inc(head_sq, 1)

            def head_rms(d_half, slot):
                act.wait_ge(head_stat, d_half + 1)
                act.activation(u_sb[:, 2 + slot, :], tp[1][:, 0:S], ACT.Ln, bias=odd[:, 7:8],
                               scale=1.0 / P).then_inc(head_rstd, 1)
                act.wait_ge(head_rstd, d_half * 2 + 1)
                act.activation(u_sb[:, 2 + slot, :], u_sb[:, 2 + slot, :], ACT.Exp, scale=-0.5)\
                   .then_inc(head_rstd, 1)

            def head_high(d_half, slot, tile):
                act.wait_ge(head_norm, d_half + 1)
                act.copy(act_hi[:, tile, :], u_sb[:, slot, :]).then_inc(mix_hi, 1)

            def evac_qk(c, slot, to):
                act.wait_ge(used, c + 1)
                act.mul(proj[:, 2 * to, :], pj[slot][:, 0:S], 0.125)
                act.copy(proj[:, 2 * to + 1, :], pj[slot][:, S:2 * S]).then_inc(bank_free, 1)

            def evac_v(c, slot, half):
                act.wait_ge(used, c + 1)
                if half is not None:
                    act.wait_ge(pv_done, half + 1)
                act.copy(vtok[:, :, :], pj[slot][:, :].rearrange("p (b f) -> p b f", b=2)).then_inc(bank_free, 1)

            load_tables(EXP_AND_LN)
            act.wait_ge(setup_in, 32)
            act.wait_ge(x_in, 16)
            for t in range(4):
                u = t
                squares(u, x[:, 2 * t:2 * t + 2, :].rearrange("p a b -> p (a b)"), 2 * S, u % 2)
            for c in range(RING):
                split_hi(c, c, SIZES[c], 0)
            for l in range(2):
                act.wait_ge(credits, 1)
                act.activation(odd[:, 2 * l:2 * l + 2], odd[:, 2 * l:2 * l + 2], ACT.Exp).then_inc(credits, 1)

            half = s_half = d_half = b_half = ffn = app = 0
            layer = 0
            prev = "x"
            for kind, c0, n in STAGES:
                if kind in ("da", "sb", "sw", "mix"):
                    groups = 2 if kind == "mix" else 4
                    rms(SUM_UNITS[prev][2])
                    split_h(app)
                    app += 1
                    lead = 0
                    if kind == "mix":
                        for k in range(2):
                            act.wait_ge(used, c0 + k + 1)
                            act.copy(u_sb[:, 2 * k:2 * k + 2, :].rearrange("p a b -> p (a b)"),
                                     pj[slot_of(c0, k)][:, :]).then_inc(bank_free, 1)
                            next_split(c0, k)
                        lead = 2
                    g0 = c0 + lead

                    if kind in ("da", "mix"):
                        first_tile = 0 if kind == "da" else 4
                        maps = 1 if kind == "da" else 2
                        da = kind == "da"

                        def group(i, more):
                            q, s, d, t = (i * 2 + half, i * 2 + s_half, i * 2 + d_half, i * 2 + first_tile)
                            at = i * RING + (g0 + RING)
                            reg = i if not isinstance(i, int) else None
                            off = g0 + RING + (i * RING if isinstance(i, int) else 0)
                            exps(s + 1, 1, 0)
                            if more:
                                evac_qk(at, slot_of(g0, 0), 0)
                            copy_probT(s, 0, maps)
                            head_squares(q, d, 0) if da else mix_high(q, t)
                            if more:
                                next_split(off, 0, reg)
                            if da:
                                head_rms(d, 0)
                            if more:
                                evac_qk(at + 1, slot_of(g0, 1), 1)
                            copy_probT(s + 1, 1, maps)
                            if da:
                                head_high(d, 0, t)
                            if more:
                                next_split(off, 1, reg)
                            head_squares(q + 1, d + 1, 1) if da else mix_high(q + 1, t + 1)
                            if more:
                                exps(s + 2, 0, 0)
                                evac_v(at + 2, slot_of(g0, 2), q + 1)
                            if da:
                                head_rms(d + 1, 1)
                            if more:
                                next_split(off, 2, reg)
                            if da:
                                head_high(d + 1, 1, t + 1)

                        evac_qk(g0, slot_of(g0, 0), 0)
                        next_split(g0, 0)
                        evac_qk(g0 + 1, slot_of(g0, 1), 1)
                        next_split(g0, 1)
                        exps(s_half, 0, 0)
                        evac_v(g0 + 2, slot_of(g0, 2), None)
                        next_split(g0, 2)
                        if groups > 2:
                            with act.Fori(0, groups - 1) as i:
                                group(i, True)
                        else:
                            group(0, True)
                        group(groups - 1, False)
                        half += 2 * groups
                        s_half += 2 * groups
                        if kind == "da":
                            d_half += 2 * groups
                    elif kind == "sb":
                        def logs(b, slot):
                            act.wait_ge(scores_done, b + (half + slot + 1))
                            for m in range(2):
                                act.activation(prob[:, slot, m, :], (sc, tp)[slot][m][:, 0:CAUSAL], ACT.Abs)\
                                   .then_inc(log_done, 1)
                            for m in range(2):
                                act.wait_ge(log_done, (b + slot) * 6 + m + 1)
                                act.activation(prob[:, slot, m, :], prob[:, slot, m, :], ACT.Exp, scale=-1.0)\
                                   .then_inc(log_done, 1)
                            for m in range(2):
                                act.wait_ge(log_done, (b + slot) * 6 + m + 3)
                                act.activation(prob[:, slot, m, :], prob[:, slot, m, :], ACT.Ln, bias=1.0)\
                                   .then_inc(log_done, 1)

                        def a_exps(b, slot):
                            act.wait_ge(cum_done, b + slot + 1)
                            bank = (sc, tp)[slot]
                            for m in range(2):
                                act.activation(probT[:, slot, m, :], bank[m][:, 0:CAUSAL], ACT.Exp)\
                                   .then_inc(a_exp, 1)

                        def group(i, more):
                            b, q = i * 2, i * 2 + half
                            at = i * RING + (g0 + RING)
                            reg = i if not isinstance(i, int) else None
                            off = g0 + RING + (i * RING if isinstance(i, int) else 0)
                            logs(b, 0)
                            logs(b, 1)
                            if more:
                                evac_qk(at, slot_of(g0, 0), 0)
                            a_exps(b, 0)
                            if more:
                                next_split(off, 0, reg)
                            a_exps(b, 1)
                            if more:
                                evac_qk(at + 1, slot_of(g0, 1), 1)
                            mix_high(q, i * 2)
                            if more:
                                next_split(off, 1, reg)
                            mix_high(q + 1, i * 2 + 1)
                            if more:
                                evac_v(at + 2, slot_of(g0, 2), q + 1)
                                next_split(off, 2, reg)

                        evac_qk(g0, slot_of(g0, 0), 0)
                        next_split(g0, 0)
                        evac_qk(g0 + 1, slot_of(g0, 1), 1)
                        next_split(g0, 1)
                        evac_v(g0 + 2, slot_of(g0, 2), None)
                        next_split(g0, 2)
                        with act.Fori(0, groups - 1) as i:
                            group(i, True)
                        group(groups - 1, False)
                        half += 2 * groups
                    else:
                        def evac_kv(t):
                            act.wait_ge(used, c0 + 3 * t + 1)
                            bank = pj[slot_of(c0, 0)]
                            act.copy((proj[:, 4, :], u_sb[:, 0, :])[t], bank[:, 0:S])
                            act.copy(vtok[:, :, P * t:P * t + P],
                                     bank[:, S:2 * S].rearrange("p (b f) -> p b f", b=2)).then_inc(bank_free, 1)

                        def evac_q(c, pair):
                            act.wait_ge(used, c + 1)
                            act.mul(proj[:, 2 * pair:2 * pair + 2, :].rearrange("p a b -> p (a b)"),
                                    pj[c % RING][:, :], 0.125).then_inc(bank_free, 1)

                        evac_kv(0)
                        next_split(c0, 0)
                        evac_q(c0 + 1, 0)
                        exps(s_half, 0, 1)
                        next_split(c0, 1)
                        evac_q(c0 + 2, 1)
                        exps(s_half + 1, 1, 2)
                        next_split(c0, 2)
                        for j in range(8):
                            q, s = half + j, s_half + j
                            copy_probT(s, j % 2, 2)
                            if j == 0:
                                evac_kv(1)
                            elif j < 3:
                                evac_q(c0 + 3 + j, j - 1)
                            if j < 6:
                                exps(s + 2, j % 2, j + 3)
                            mix_high(q, j)
                            if j < 3:
                                next_split(c0 + 3, j)
                        half += 8
                        s_half += 8
                    if kind == "mix":
                        k = n - 1
                        act.wait_ge(used, c0 + k + 1)
                        for g in range(4):
                            bank = (pj[slot_of(c0, k)], tp[0])[g // 2]
                            act.mul(act_hi[:, g, :], bank[:, g % 2 * S:g % 2 * S + S],
                                    param("pool_scale", g)).then_inc(mix_hi, 1)
                        next_split(c0, k)
                elif kind == "wo":
                    name = f"wo{layer}"
                    u0 = SUM_UNITS[name][0]
                    for k in range(4):
                        if layer < 4:
                            act.wait_ge(bank_free, RING + c0 + k + 1)
                            squares(u0 + k, x[:, 2 * k:2 * k + 2, :].rearrange("p a b -> p (a b)"), 2 * S,
                                    (u0 + k) % 2)
                        else:
                            act.wait_ge(used, c0 + k + 1)
                            act.copy(tmp[:, 2 * k:2 * k + 2, :].rearrange("p a b -> p (a b)"),
                                     pj[slot_of(c0, k)][:, :]).then_inc(bank_free, 1)
                            act.wait_ge(acc_done, u0 + k + 1)
                            act.wait_ge(bank_free, RING + c0 + k + 1)
                            act.activation(sq[:, (u0 + k) % 2, :],
                                           tmp[:, 2 * k:2 * k + 2, :].rearrange("p a b -> p (a b)"),
                                           ACT.Square).then_inc(sq_ready, 1)
                        if k < 3:
                            next_split(c0, k)
                    rms(SUM_UNITS[name][2])
                    if layer == 4:
                        next_split(c0, 3)
                        u0 = SUM_UNITS["res_a"][0]
                        for k in range(4):
                            act.wait_ge(x_ready, 4 + k + 1)
                            squares(u0 + k, x[:, 2 * k:2 * k + 2, :].rearrange("p a b -> p (a b)"), 2 * S,
                                    (u0 + k) % 2)
                        rms(SUM_UNITS["res_a"][2])
                        split_h(app)
                    else:
                        split_h(app)
                        next_split(c0, 3)
                    app += 1
                elif kind == "up":
                    convs = 2 if ffn < 4 else 1

                    def step(j, c, slot, split):
                        n_ = j + ffn * FT
                        act.wait_ge(used, c + 1)
                        act.wait_ge(act_free, n_ + 1)
                        for v in range(convs):
                            bank, to = ((pj, cgate), (val_bank, cval))[v]
                            at = j * 8 + (4 * v + PARAM["conv"] + ffn * FT * 8) if ffn < 4 else j * 4 + PARAM["conv2"]
                            def col(k_):
                                return par[:, bass.ds(at + k_, 1)]
                            act.activation(to[:, slot, :], bank[slot][:, 0:S], ACT.Identity,
                                           bias=col(3), scale=col(2)).then_inc(conv_init, 1)
                        split()
                        act.wait_ge(conv_part, (j * 3 + (ffn * FT * 3 + 3)) if ffn < 4 else (j * 2 + (4 * FT * 3 + 2)))
                        act.activation(cgate[:, slot, :], cgate[:, slot, :],
                                       ACT.Silu if ffn < 4 else ACT.Gelu_apprx_tanh).then_inc(gated, 1)

                    turns = (n - RING) // RING
                    with act.Fori(0, turns) as i:
                        for k in range(RING):
                            step(i * RING + k, i * RING + (c0 + k), slot_of(c0, k),
                                 lambda: next_split(c0, k, i))
                    for j in range(turns * RING, n):
                        step(j, c0 + j, slot_of(c0, j), lambda: next_split(c0, j))
                    ffn += 1
                elif kind == "down":
                    load_tables(EXP_AND_LN)
                    name = f"down{layer}"
                    u0 = SUM_UNITS[name][0]
                    for k in range(DT):
                        if layer < 4:
                            act.wait_ge(bank_free, RING + c0 + k + 1)
                            squares(u0 + k, x[:, k, :], S, (u0 + k) % 2)
                        else:
                            act.wait_ge(used, c0 + k + 1)
                            act.copy(tmp[:, k, :], pj[slot_of(c0, k)][:, 0:S]).then_inc(bank_free, 1)
                            act.wait_ge(acc_done, u0 + k + 1)
                            act.wait_ge(bank_free, RING + c0 + k + 1)
                            act.activation(sq[:, (u0 + k) % 2, 0:S], tmp[:, k, :], ACT.Square)\
                               .then_inc(sq_ready, 1)
                        next_split(c0, k)
                    if layer == 3:
                        rms(SUM_UNITS[name][2])
                        u0 = SUM_UNITS["final"][0]
                        for k in range(4):
                            act.wait_ge(x_ready, k + 1)
                            squares(u0 + k, x[:, 2 * k:2 * k + 2, :].rearrange("p a b -> p (a b)"), 2 * S,
                                    (u0 + k) % 2)
                        prev = "final"
                    elif layer == 4:
                        rms(SUM_UNITS[name][2])
                        for k in range(DT):
                            act.wait_ge(hf_done, app * DT + k + 1)
                            act.copy(h_hi[:, k, :], x[:, k, :]).then_inc(h_hi_done, 1)
                        act.wait_ge(p_in, 16)
                        act.copy(act_hi[:, 0:2, :], u_sb[:, 0:2, :]).then_inc(p_hi, 1)
                    else:
                        prev = name
                    layer += 1
                else:
                    for k in range(n):
                        act.wait_ge(used, c0 + k + 1)
                        act.activation(tmp[:, 2 * k:2 * k + 2, :].rearrange("p a b -> p (a b)"),
                                       pj[slot_of(c0, k)][:, :], ACT.Sigmoid).then_inc(sig_done, 1)
                        next_split(c0, k)

        @block.vector
        def _(dve):
            steps = [0]

            def wait_step():
                dve.wait_ge(dve_step, steps[0])

            def split_lo(c, slot, width):
                dve.wait_ge(hi_ready, c + 1)
                dve.tensor_tensor(w_lo[:, slot, 0:width], w_raw[:, slot, 0:width],
                                  w_hi[:, slot, 0:width].bitcast(F32), ALU.subtract).then_inc(lo_ready, 1)

            def next_split(c0, k, i=None):
                n = c0 + k + RING
                if i is None and n >= CHUNKS:
                    return
                split_lo(n if i is None else i * RING + n, n % RING, SIZES[n])

            def add_squares(unit, first, columns):
                dve.wait_ge(sq_ready, unit + 1)
                dve.wait_ge(acc_done, unit + 2)
                a, b = columns
                n = unit % 2
                if first:
                    ins = dve.tensor_copy(acc[:, a:b], sq[:, n, 0:b - a])
                else:
                    ins = dve.tensor_tensor(acc[:, a:b], acc[:, a:b], sq[:, n, 0:b - a], ALU.add)
                ins.then_inc(acc_done, 1)

            def normalise(app, norm, gain):
                dve.wait_ge(rstd_done, norm + 1)

                def low(k):
                    dve.wait_ge(h_hi_done, app * DT + k + 1)
                    dve.tensor_tensor(h_lo[:, k, :], tmp[:, k, :], h_hi[:, k, :].bitcast(F32),
                                      ALU.subtract).then_inc(h_lo_even, 1)

                for k in range(DT):
                    dve.scalar_tensor_tensor(tmp[:, k, :], x[:, k, :], gain(k), rstd[:, :],
                                             ALU.mult, ALU.mult).then_inc(hf_done, 1)
                    if k % 2 and k > 1:
                        low(k - 3)
                low(DT - 2)

            def take_scores(half, s_half, turn, slot, sink):
                dve.wait_ge(scores_done, half + 1)
                dve.wait_ge(bias_in[slot], turn * 32 + 32)
                dve.memset(wait_mark[:, slot:slot + 1], 0.0)
                for m in range(2):
                    table = (act_hi, act_lo)[m]
                    for qb, (a, b, keys) in enumerate(((0, QB, QB), (QB, CAUSAL, S))):
                        n = 2 * m + qb
                        bias = table[:, 8 + slot, keys - 1::-1].bitcast(F32)
                        last = dve.tensor_tensor_reduce(prob[:, slot, m, a:b], sc[m][:, a:b],
                                                        bias, 1.0, NEG * 10,
                                                        ALU.add, ALU.max, small[:, slot, 0, n:n + 1])
                last.then_inc(scores_taken, 1)
                dve.wait_ge(scores_taken, s_half + 1)
                if sink is None:
                    dve.tensor_scalar(small[:, slot, 1, :], small[:, slot, 0, :], -1.0, None, ALU.mult)\
                       .then_inc(nmax_ready, 1)
                else:
                    col = param("sinks", 4 * sink, 4)
                    dve.tensor_tensor(small[:, slot, 0, :], small[:, slot, 0, :], col, ALU.max)\
                       .then_inc(dve_step, 1)
                    steps[0] += 1
                    wait_step()
                    dve.tensor_scalar(small[:, slot, 1, :], small[:, slot, 0, :], -1.0, None, ALU.mult)\
                       .then_inc(nmax_ready, 1)
                    dve.tensor_tensor(small[:, slot, 4, :], col, small[:, slot, 0, :], ALU.subtract)\
                       .then_inc(sink_shift, 1)

            def divide(s_half, slot, sink, base, lam_col=None):
                dve.wait_ge(exp_done, s_half + 1)
                done = 0

                def step(ins):
                    nonlocal done
                    done += 1
                    ins.then_inc(dve_step, 1)
                    dve.wait_ge(dve_step, base + done)

                if sink:
                    step(dve.tensor_tensor(small[:, slot, 2, :], small[:, slot, 2, :], small[:, slot, 4, :], ALU.add))
                step(dve.reciprocal(small[:, slot, 3, :], small[:, slot, 2, :]))
                spans = ((0, QB), (QB, CAUSAL))
                if lam_col is None:
                    for m in range(2):
                        for qb, (a, b) in enumerate(spans):
                            n = 2 * m + qb
                            last = dve.tensor_scalar(prob[:, slot, m, a:b], prob[:, slot, m, a:b],
                                                     small[:, slot, 3, n:n + 1], None, ALU.mult)
                else:
                    step(dve.tensor_scalar(small[:, slot, 4, 0:2], small[:, slot, 3, 2:4], lam_col, None, ALU.mult))
                    for qb, (a, b) in enumerate(spans):
                        ins = dve.tensor_scalar(prob[:, slot, 1, a:b], prob[:, slot, 1, a:b],
                                                small[:, slot, 4, qb:qb + 1], None, ALU.mult)
                    step(ins)
                    for qb, (a, b) in enumerate(spans):
                        last = dve.scalar_tensor_tensor(prob[:, slot, 0, a:b], prob[:, slot, 0, a:b],
                                                        small[:, slot, 3, qb:qb + 1], prob[:, slot, 1, a:b],
                                                        ALU.mult, ALU.add)
                last.then_inc(probs_done, 1)
                return done

            def add_normed(k, gain, signal):
                dve.scalar_tensor_tensor(tmp[:, 8 + k % 4, :], tmp[:, k, :], param(gain, k),
                                         rstd[:, :], ALU.mult, ALU.mult).then_inc(dve_step, 1)
                steps[0] += 1
                wait_step()
                ins = dve.tensor_tensor(x[:, k, :], x[:, k, :], tmp[:, 8 + k % 4, :], ALU.add)
                if signal is not None:
                    ins.then_inc(signal, 1)

            def mix_low(half, tile):
                dve.wait_ge(mix_hi, half + 1)
                dve.tensor_tensor(act_lo[:, tile, :], ov[:, 0:S], act_hi[:, tile, :].bitcast(F32),
                                  ALU.subtract).then_inc(mix_lo, 1)

            def head_normed(d_half, slot, da_layer):
                dve.wait_ge(head_rstd, d_half * 2 + 2)
                dve.scalar_tensor_tensor(u_sb[:, slot, :], u_sb[:, slot, :], odd[:, 4 + da_layer:5 + da_layer],
                                         u_sb[:, 2 + slot, :], ALU.mult, ALU.mult).then_inc(head_norm, 1)

            def head_low(half, slot, tile):
                dve.wait_ge(mix_hi, half + 1)
                dve.tensor_tensor(act_lo[:, tile, :], u_sb[:, slot, :], act_hi[:, tile, :].bitcast(F32),
                                  ALU.subtract).then_inc(mix_lo, 1)

            for b, free in enumerate([bank_free] * RING + [act_free] * RING + [acc_done] * 2):
                dve.memset(small[:, b // 5, b % 5, :], 0.0).then_inc(free, 1)
            dve.memset(odd[:, 7:8], EPS).then_inc(dve_step, 1)
            steps[0] += 1
            wait_step()
            dve.wait_ge(x_in, 16)
            for t in range(4):
                add_squares(t, t == 0, (0, 2 * S))
            for c in range(RING):
                split_lo(c, c, SIZES[c])
            dve.wait_ge(tab_in, 64)
            lam_sb = tmp[:, 8:10, :]
            for l in range(2):
                for a in range(2):
                    last = dve.tensor_tensor_reduce(tmp[:, 10, 0:64], lam_sb[:, l, 128 * a:128 * a + 64],
                                                    lam_sb[:, l, 128 * a + 64:128 * a + 128], 1.0, 0.0,
                                                    ALU.mult, ALU.add, odd[:, 2 * l + a:2 * l + a + 1])
                    last.then_inc(dve_step, 1)
                    steps[0] += 1
                    wait_step()
            dve.memset(tmp[:, 10, 0:64], 0.0).then_inc(credits, 1)
            dve.wait_ge(credits, 3)
            for l in range(2):
                dve.tensor_tensor(odd[:, 2 * l:2 * l + 1], odd[:, 2 * l + 1:2 * l + 2], odd[:, 2 * l:2 * l + 1],
                                  ALU.subtract).then_inc(dve_step, 1)
                dve.tensor_scalar(odd[:, 4 + l:5 + l], param("subln", l), 1.0 - lambda_init(3 * l), None,
                                  ALU.mult).then_inc(dve_step, 1)
                steps[0] += 2
                wait_step()
                dve.tensor_scalar(odd[:, 2 * l:2 * l + 1], odd[:, 2 * l:2 * l + 1], -lambda_init(3 * l), None,
                                  ALU.add).then_inc(dve_step, 1)
                steps[0] += 1
                wait_step()
            for t in range(3):
                dve.wait_ge(vec_psum, t + 1)
                dve.tensor_copy(u_sb[0:16, 0:2, :].rearrange("p a b -> p (a b)")[:, 0:NVEC] if t == 0 else
                                (u_sb[0:16, 2:4, :].rearrange("p a b -> p (a b)")[:, 0:NVEC] if t == 1 else
                                 tmp[0:16, 10:12, :].rearrange("p a b -> p (a b)")[:, 0:NVEC]),
                                banks[3 + t][0:16, 0:NVEC]).then_inc(vec_sb, 1)

            half = s_half = d_half = ffn = app = 0
            layer = 0
            da_layer = 0
            prev = "x"
            for kind, c0, n in STAGES:
                if kind in ("da", "sb", "sw", "mix"):
                    groups = 2 if kind == "mix" else 4
                    gain_name = "attn_norm" if kind != "mix" else "mix_pre"
                    if layer == 0:
                        dve.wait_ge(vec_out, 48)
                    normalise(app, SUM_UNITS[prev][2],
                              lambda k: param(gain_name, k + (DT * layer if layer < 4 else 0)))
                    app += 1
                    lead = 0
                    if kind == "mix":
                        for k in range(2):
                            next_split(c0, k)
                        lead = 2
                    g0 = c0 + lead
                    if kind in ("da", "mix"):
                        per = 3 if kind == "da" else 1
                        lam_col = odd[:, 2 * da_layer:2 * da_layer + 1] if kind == "da" else None
                        base = steps[0]

                        first_tile = 0 if kind == "da" else 4
                        da = kind == "da"

                        def group(i, more):
                            q, s, d, t = (i * 2 + half, i * 2 + s_half, i * 2 + d_half, i * 2 + first_tile)
                            b = i * (2 * per) + base
                            reg = i if not isinstance(i, int) else None
                            off = g0 + RING + (i * RING if isinstance(i, int) else 0)
                            assert divide(s, 0, False, b, lam_col) == per
                            take_scores(q + 1, s + 1, i + s_half // 2, 1, None)
                            divide(s + 1, 1, False, b + per, lam_col)
                            if more:
                                next_split(off, 0, reg)
                            if da:
                                head_normed(d, 0, da_layer)
                                head_low(q, 0, t)
                            else:
                                mix_low(q, t)
                            if more:
                                next_split(off, 1, reg)
                                take_scores(q + 2, s + 2, i + (s_half // 2 + 1), 0, None)
                            if da:
                                head_normed(d + 1, 1, da_layer)
                            else:
                                mix_low(q + 1, t + 1)
                            if more:
                                next_split(off, 2, reg)
                            if da:
                                head_low(q + 1, 1, t + 1)

                        next_split(g0, 0)
                        next_split(g0, 1)
                        take_scores(half, s_half, s_half // 2, 0, None)
                        next_split(g0, 2)
                        if groups > 2:
                            with dve.Fori(0, groups - 1) as i:
                                group(i, True)
                        else:
                            group(0, True)
                        group(groups - 1, False)
                        steps[0] += 2 * per * groups
                        half += 2 * groups
                        s_half += 2 * groups
                        if kind == "da":
                            d_half += 2 * groups
                            da_layer += 1
                    elif kind == "sb":
                        def softplus(b, slot):
                            for m in range(2):
                                bank = (sc, tp)[slot]
                                dve.wait_ge(log_done, (b + slot) * 6 + m + 5)
                                dve.scalar_tensor_tensor(prob[:, slot, m, :], bank[m][:, 0:CAUSAL], 0.0,
                                                         prob[:, slot, m, :], ALU.max, ALU.add)\
                                   .then_inc(sp_done, 1)

                        def group(i, more):
                            b, q = i * 2, i * 2 + half
                            reg = i if not isinstance(i, int) else None
                            off = g0 + RING + (i * RING if isinstance(i, int) else 0)
                            softplus(b, 0)
                            softplus(b, 1)
                            if more:
                                next_split(off, 0, reg)
                                next_split(off, 1, reg)
                            mix_low(q, i * 2)
                            mix_low(q + 1, i * 2 + 1)
                            if more:
                                next_split(off, 2, reg)

                        for k in range(3):
                            next_split(g0, k)
                        with dve.Fori(0, groups - 1) as i:
                            group(i, True)
                        group(groups - 1, False)
                        half += 2 * groups
                    else:
                        def take(j):
                            take_scores(half + j, s_half + j, (s_half + j) // 2, j % 2, j)

                        next_split(c0, 0)
                        take(0)
                        next_split(c0, 1)
                        take(1)
                        steps[0] += divide(s_half, 0, True, steps[0])
                        next_split(c0, 2)
                        steps[0] += divide(s_half + 1, 1, True, steps[0])
                        for j in range(8):
                            if j < 6:
                                take(j + 2)
                            mix_low(half + j, j)
                            if j < 6:
                                steps[0] += divide(s_half + j + 2, j % 2, True, steps[0])
                            if j < 3:
                                next_split(c0 + 3, j)
                        half += 8
                        s_half += 8
                    if kind == "mix":
                        k = n - 1
                        dve.wait_ge(mix_hi, half + 4)
                        for g in range(4):
                            bank = (pj[slot_of(c0, k)], tp[0])[g // 2]
                            last = dve.scalar_tensor_tensor(act_lo[:, g, :], bank[:, g % 2 * S:g % 2 * S + S],
                                                            param("pool_scale", g), act_hi[:, g, :].bitcast(F32),
                                                            ALU.mult, ALU.subtract)
                        last.then_inc(bank_free, 1)
                        next_split(c0, k)
                elif kind == "wo":
                    name = f"wo{layer}"
                    u0 = SUM_UNITS[name][0]
                    for k in range(4):
                        if layer < 4:
                            xk = x[:, 2 * k:2 * k + 2, :].rearrange("p a b -> p (a b)")
                            dve.wait_ge(used, c0 + k + 1)
                            dve.tensor_tensor(xk, pj[slot_of(c0, k)][:, :], xk, ALU.add).then_inc(bank_free, 1)
                        add_squares(u0 + k, k == 0, (0, 2 * S))
                        if k < 3:
                            next_split(c0, k)
                    if layer < 4:
                        normalise(app, SUM_UNITS[name][2], lambda k: param("ffn_norm", k + DT * layer))
                        next_split(c0, 3)
                    else:
                        next_split(c0, 3)
                        dve.wait_ge(rstd_done, SUM_UNITS[name][2] + 1)
                        for k in range(DT):
                            add_normed(k, "mix_post", x_ready if k % 2 else None)
                        for t in range(4):
                            add_squares(SUM_UNITS["res_a"][0] + t, t == 0, (0, 2 * S))
                        normalise(app, SUM_UNITS["res_a"][2], lambda k: param("ffn_pre", k))
                    app += 1
                elif kind == "up":
                    def step(j, c, slot, split):
                        n_ = j + ffn * FT
                        convs = 2 if ffn < 4 else 1
                        at = j * 8 + (PARAM["conv"] + ffn * FT * 8) if ffn < 4 else j * 4 + PARAM["conv2"]
                        init = j * 2 + ffn * FT * 2 if ffn < 4 else j + 4 * FT * 2
                        part = j * 3 + ffn * FT * 3 if ffn < 4 else j * 2 + 4 * FT * 3

                        def tap(v, lag):
                            bank, to = ((pj, cgate), (val_bank, cval))[v]
                            return dve.scalar_tensor_tensor(
                                to[:, slot, lag:S], bank[slot][:, 0:S - lag],
                                par[:, bass.ds(at + (4 * v + 2 - lag), 1)], to[:, slot, lag:S],
                                ALU.mult, ALU.add)

                        for v in range(convs):
                            dve.wait_ge(conv_init, init + (v + 1))
                            tap(v, 1).then_inc(conv_part, 1)
                        dve.wait_ge(conv_part, part + 1)
                        tap(0, 2).then_inc(conv_part, 1)
                        if convs == 2:
                            dve.wait_ge(conv_part, part + 2)
                            tap(1, 2).then_inc(bank_free, 1)
                        split()
                        dve.wait_ge(gated, n_ + 1)
                        if convs == 2:
                            dve.wait_ge(bank_free, c + (RING + 1))
                            dve.tensor_tensor(cval[:, slot, :], cgate[:, slot, :], cval[:, slot, :],
                                              ALU.mult).then_inc(prod_done, 1)
                        else:
                            dve.tensor_tensor(cval[:, slot, :], val_bank[slot][:, 0:S], cgate[:, slot, :],
                                              ALU.mult).then_inc(bank_free, 1)

                    turns = (n - RING) // RING
                    with dve.Fori(0, turns) as i:
                        for k in range(RING):
                            step(i * RING + k, i * RING + (c0 + k), slot_of(c0, k),
                                 lambda: next_split(c0, k, i))
                    for j in range(turns * RING, n):
                        step(j, c0 + j, slot_of(c0, j), lambda: next_split(c0, j))
                    ffn += 1
                elif kind == "down":
                    name = f"down{layer}"
                    u0 = SUM_UNITS[name][0]
                    for k in range(DT):
                        if layer < 4:
                            dve.wait_ge(used, c0 + k + 1)
                            dve.tensor_tensor(x[:, k, :], pj[slot_of(c0, k)][:, 0:S], x[:, k, :], ALU.add)\
                               .then_inc(bank_free, 1)
                        add_squares(u0 + k, k < 2, (k % 2 * S, k % 2 * S + S))
                        next_split(c0, k)
                    if layer == 3:
                        dve.wait_ge(rstd_done, SUM_UNITS[name][2] + 1)
                        for k in range(DT):
                            ins = dve.scalar_tensor_tensor(x[:, k, :], x[:, k, :], param("final_norm", k),
                                                           rstd[:, :], ALU.mult, ALU.mult)
                            if k % 2:
                                ins.then_inc(x_ready, 1)
                        for t in range(4):
                            add_squares(SUM_UNITS["final"][0] + t, t == 0, (0, 2 * S))
                        prev = "final"
                    elif layer == 4:
                        dve.wait_ge(rstd_done, SUM_UNITS[name][2] + 1)
                        for k in range(DT):
                            add_normed(k, "ffn_post", hf_done)
                        for k in range(0, DT, 2):
                            dve.wait_ge(h_hi_done, app * DT + k + 1)
                            dve.tensor_tensor(h_lo[:, k, :], x[:, k, :], h_hi[:, k, :].bitcast(F32),
                                              ALU.subtract).then_inc(h_lo_even, 1)
                        dve.wait_ge(p_hi, 1)
                        dve.tensor_tensor(act_lo[:, 0:2, :], u_sb[:, 0:2, :], act_hi[:, 0:2, :].bitcast(F32),
                                          ALU.subtract).then_inc(p_lo, 1)
                    else:
                        prev = name
                    layer += 1
                else:
                    for k in range(n):
                        next_split(c0, k)
                        both = tmp[:, 2 * k:2 * k + 2, :].rearrange("p a b -> p (a b)")
                        xk = x[:, 2 * k:2 * k + 2, :].rearrange("p a b -> p (a b)")
                        dve.wait_ge(sig_done, k + 1)
                        dve.tensor_tensor(both, val_bank[k % 3][:, :], both, ALU.mult).then_inc(bank_free, 1)
                        dve.wait_ge(bank_free, RING + c0 + k + 1)
                        dve.tensor_tensor(xk, xk, both, ALU.add).then_inc(out_ready, 1)

        @block.gpsimd
        def _(pool):
            def bias_dma(table, s, slot, pair, free=True):
                if free:
                    pool.wait_ge(scores_taken, s - 1)
                for m, to in enumerate((act_hi, act_lo)):
                    src = bass.AP(tensor=vec_dram, offset=pair * (2 * NVEC) + (table * 16 + m) * NVEC,
                                  ap=[[1, P], [1, S]])
                    pool.dma_start(to[:, 8 + slot, :].bitcast(F32), src).then_inc(bias_in[slot], 16)

            def low_odd(app, source):
                for k in range(1, DT, 2):
                    pool.wait_ge(h_hi_done, app * DT + k + 1)
                    pool.tensor_tensor(h_lo[:, k, :], source[:, k, :], h_hi[:, k, :].bitcast(F32),
                                       ALU.subtract).then_inc(h_lo_odd, 1)

            own = [0]

            def step(ins):
                own[0] += 1
                ins.then_inc(pooled, 1)
                pool.wait_ge(pooled, own[0])

            for t, at in enumerate((6, 0)):
                pool.dma_start(tmp[0:33, at:at + 2, :].rearrange("p a b -> p (a b)")[:, 0:NVEC], onehot[t])\
                    .then_inc(tab_in, 16)
            pool.dma_start(tmp[0:33, 5, 0:48], tables).then_inc(tab_in, 16)
            pool.dma_start(tmp[:, 8:10, :], lam).then_inc(tab_in, 16)
            pool.wait_ge(vec_sb, 3)
            for t, src in enumerate((u_sb[0:16, 0:2, :], u_sb[0:16, 2:4, :], tmp[0:16, 10:12, :])):
                pool.dma_start(vec_dram[t], src.rearrange("p a b -> p (a b)")[:, 0:NVEC]).then_inc(vec_out, 16)
            pool.wait_ge(vec_out, 48)

            s_half = ffn = app = layer = 0
            for kind, c0, n in STAGES:
                if kind in ("da", "sw", "mix"):
                    table = {"da": 0, "sw": 1, "mix": 2}[kind]
                    halves = 4 if kind == "mix" else 8
                    if c0:
                        pool.wait_ge(used, c0)
                    for b in range(2):
                        bias_dma(table, s_half + b, b, b, free=s_half > 0)
                    low_odd(app, tmp)
                    app += 1
                    if kind == "mix":
                        pool.wait_ge(bank_free, RING + c0 + 2)
                        for g, w in enumerate(WINDOWS):
                            src, k, at = u_sb[:, g, :], 1, 0
                            while k < w:
                                dst = sq[:, 0, at * S:at * S + S]
                                pool.tensor_copy(dst[:, 0:k], src[:, 0:k])
                                step(pool.tensor_tensor(dst[:, k:S], src[:, k:S], src[:, 0:S - k], ALU.add))
                                src, k, at = dst, 2 * k, 1 - at
                            dst = sq[:, 1, 0:S]
                            pool.tensor_tensor(dst[:, 0:16], src[:, 0:16], param("inv_count", 16 * g, 16), ALU.mult)
                            step(pool.tensor_scalar(dst[:, 16:S], src[:, 16:S], 1.0 / w, None, ALU.mult))
                            mean = sq[:, 1, S:2 * S]
                            step(pool.tensor_tensor(mean, dst, u_sb[:, g, :], ALU.subtract))
                            step(pool.tensor_copy(act_hi[:, 16 + g, :], mean))
                            step(pool.tensor_tensor(act_lo[:, 16 + g, :], mean,
                                                    act_hi[:, 16 + g, :].bitcast(F32), ALU.subtract))
                    if kind == "da":
                        with pool.Fori(1, halves // 2) as i:
                            for b in range(2):
                                bias_dma(table, i * 2 + (s_half + b), b, i * 2 + b)
                    else:
                        for h in range(2, halves):
                            bias_dma(table, s_half + h, h % 2, h)
                    s_half += halves
                elif kind == "sb":
                    low_odd(app, tmp)
                    app += 1

                    def mask(buffer, slot, m):
                        v = buffer[:, slot, m, :].rearrange("p (b c) -> p b c", c=P)[:, 0:3:2, :]
                        return pool.affine_select(out=v, in_=v, compare_op=ALU.is_gt, fill=0.0, base=0,
                                                  pattern=[[0, 2], [1, P]], channel_multiplier=-1)

                    for i in range(4):
                        for slot in range(2):
                            for m in range(2):
                                pool.wait_ge(sp_done, i * 4 + (2 * slot + m + 1))
                                mask(prob, slot, m).then_inc(sp_masked, 1)
                        for slot in range(2):
                            for m in range(2):
                                pool.wait_ge(a_exp, i * 4 + (2 * slot + m + 1))
                                mask(probT, slot, m).then_inc(a_masked, 1)
                elif kind == "wo":
                    low_odd(app, tmp)
                    app += 1
                elif kind == "up":
                    def split_act(j, c, slot):
                        n_ = j + ffn * FT
                        if ffn < 4:
                            pool.wait_ge(prod_done, n_ + 1)
                        else:
                            pool.wait_ge(bank_free, c + (RING + 1))
                        pool.tensor_copy(act_hi[:, bass.ds(j, 1), :].squeeze(1) if not isinstance(j, int) else
                                         act_hi[:, j, :], cval[:, slot, :]).then_inc(act_hi_done, 1)
                        pool.wait_ge(act_hi_done, n_ + 1)
                        pool.tensor_tensor(act_lo[:, j, :], cval[:, slot, :], act_hi[:, j, :].bitcast(F32),
                                           ALU.subtract).then_inc(act_free, 1)

                    with pool.Fori(0, n // RING) as i:
                        for k in range(RING):
                            split_act(i * RING + k, i * RING + (c0 + k), slot_of(c0, k))
                    for j in range(n // RING * RING, n):
                        split_act(j, c0 + j, slot_of(c0, j))
                    ffn += 1
                elif kind == "down":
                    if layer == 4:
                        pool.dma_start(u_sb[:, 0:2, :], pT).then_inc(p_in, 16)
                        low_odd(app, x)
                    layer += 1

        @block.tensor
        def _(pe):
            def product(dst, weights, moving, start=True, stop=True, shared=False):
                for k, ((wh, wl), (xh, xl)) in enumerate(zip(weights, moving)):
                    first, last = start and k == 0, stop and k == len(weights) - 1
                    pe.matmul(dst, wh, xh, start=first, stop=False, skip_group_check=shared)
                    pe.matmul(dst, wh, xl, start=False, stop=False, skip_group_check=shared)
                    done = pe.matmul(dst, wl, xh, start=False, stop=last, skip_group_check=shared)
                return done

            def chunk_ready(c):
                pe.wait_ge(lo_ready, c + 1)
                pe.wait_ge(bank_free, c + 1)

            def w_tile(slot, k, width, at):
                a = k * width + at
                return w_hi[:, slot, a:a + P], w_lo[:, slot, a:a + P]

            def h_tile(k, a=0, b=S):
                return h_hi[:, k, a:b], h_lo[:, k, a:b]

            def outputs(slot, tile, dst, app=None):
                for k in range(DT):
                    if app is not None:
                        pe.wait_ge(h_lo_odd if k % 2 else h_lo_even, app * (DT // 2) + k // 2 + 1)
                    done = product(dst, [w_tile(slot, k, 2 * P, tile * P)], [h_tile(k)],
                                   start=k == 0, stop=k == DT - 1)
                return done

            def project(c, slot, app=None, between=None):
                chunk_ready(c)
                outputs(slot, 0, pj[slot][:, 0:S], app)
                if between:
                    between()
                outputs(slot, 1, pj[slot][:, S:2 * S]).then_inc(used, 1)

            def project_half(c, slot, tile):
                if tile == 0:
                    chunk_ready(c)
                done = outputs(slot, tile, pj[slot][:, tile * S:tile * S + S])
                if tile:
                    done.then_inc(used, 1)

            def out_part(c, slot, tile, a, b):
                if a == 0 and tile == 0:
                    chunk_ready(c)
                done = product(pj[slot][:, tile * S:tile * S + S],
                               [w_tile(slot, f, 2 * P, tile * P) for f in range(a, b)],
                               [(act_hi[:, f, :], act_lo[:, f, :]) for f in range(a, b)],
                               start=a == 0 and tile == 0, stop=b == DT, shared=True)
                if tile and b == DT:
                    done.then_inc(used, 1)

            def project_tokens(slot, at, a, width, blocks=(0, 1)):
                for b in blocks:
                    done = product(pj[slot][:, at + b * width:at + (b + 1) * width],
                                   [h_tile(k, b * P, b * P + P) for k in range(DT)],
                                   [(w_hi[:, slot, k * S + a:k * S + a + width],
                                     w_lo[:, slot, k * S + a:k * S + a + width]) for k in range(DT)])
                if blocks[-1] == 1:
                    done.then_inc(used, 1)

            def project_v(c, slot):
                chunk_ready(c)
                project_tokens(slot, 0, 0, 2 * P)

            def statistic(norm, units):
                pe.wait_ge(acc_done, 2 + units)
                pe.matmul(ov[:, 0:S], ones, acc[:, 0:S], start=True, stop=False)
                pe.matmul(ov[:, 0:S], ones, acc[:, S:2 * S], start=False, stop=True).then_inc(stat_done, 1)

            def stat_of(name):
                u0, n, norm = SUM_UNITS[name]
                statistic(norm, u0 + n)

            def scores(s_half, q_tile, k_tile):
                pe.wait_ge(scores_taken, s_half)
                for m in range(2):
                    q = proj[64 * m:64 * m + 64, q_tile, :]
                    k = (u_sb[64 * m:64 * m + 64, 0, :] if k_tile is None else
                         proj[64 * m:64 * m + 64, k_tile, :])
                    pe.matmul(sc[m][:, 0:QB], q[:, 0:QB], k[:, 0:QB], start=True, stop=True)
                    done = pe.matmul(sc[m][:, QB:CAUSAL], q[:, QB:S], k, start=True, stop=True)
                done.then_inc(scores_done, 1)

            def transposes(s_half, slot, maps):
                pe.wait_ge(probs_done, s_half + 1)
                pe.wait_ge(probT_done, s_half)
                for m in range(maps):
                    for b in range(3):
                        done = pe.transpose(tp[m][:, b * P:b * P + P], prob[:, slot, m, b * P:b * P + P], ident)
                done.then_inc(trans_done, 1)

            def heads(half, slot, columns):
                pe.wait_ge(mix_lo, half)
                n = P // len(columns)
                for m, a in enumerate(columns):
                    to = ov[n * m:n * m + n, :]
                    pe.matmul(to[:, 0:S], vtok[:, 0, a:a + n], probT[:, slot, m, 0:S], start=True, stop=False)
                    done = pe.matmul(to[:, QB:S], vtok[:, 1, a:a + n], probT[:, slot, m, S:CAUSAL],
                                     start=False, stop=True)
                done.then_inc(pv_done, 1)

            pe.wait_ge(tab_in, 64)
            for t in range(3):
                pe.matmul(banks[3 + t][0:16, 0:NVEC], tmp[0:33, 5, 16 * t:16 * t + 16],
                          tmp[0:33, (6, 0, 6)[t]:(8, 2, 8)[t], :].rearrange("p a b -> p (a b)")[:, 0:NVEC],
                          start=True, stop=True).then_inc(vec_psum, 1)
            pe.wait_ge(setup_in, 32)
            stat_of("x")

            half = s_half = d_half = ffn = app = layer = 0
            for kind, c0, n in STAGES:
                if kind in ("da", "mix"):
                    groups = 2 if kind == "mix" else 4
                    lead = 2 if kind == "mix" else 0
                    g0 = c0 + lead
                    for k in range(lead):
                        project(c0 + k, slot_of(c0, k), app if k == 0 else None)
                    project(g0, slot_of(g0, 0), app if lead == 0 else None)
                    project(g0 + 1, slot_of(g0, 1))
                    chunk_ready(g0 + 2)
                    project_tokens(slot_of(g0, 2), 0, 0, 2 * P, (0,))
                    pe.wait_ge(bank_free, RING + g0 + 1)
                    scores(s_half, 0, 1)
                    project_tokens(slot_of(g0, 2), 0, 0, 2 * P, (1,))
                    da = kind == "da"
                    maps = 1 if da else 2
                    cols = [[0], [P]] if da else [[0, 64], [P, P + 64]]

                    def head_statistic(d, slot):
                        pe.wait_ge(head_sq, d + 1)
                        pe.wait_ge(head_rstd, d * 2)
                        pe.matmul(tp[1][:, 0:S], ones, u_sb[:, 2 + slot, :], start=True, stop=True)\
                          .then_inc(head_stat, 1)

                    def beside(i, more, k, part):
                        at, slot = i * RING + (g0 + RING) + k, slot_of(g0, k)
                        if more:
                            if k < 2:
                                project_half(at, slot, part)
                            else:
                                if part == 0:
                                    chunk_ready(at)
                                project_tokens(slot, 0, 0, 2 * P, (part,))
                        elif da:
                            if part == 0:
                                pe.wait_ge(mix_lo, half + filled[k])
                            out_part(at, slot, part, 0, filled[k])

                    def group(i, more):
                        q, s, d = i * 2 + half, i * 2 + s_half, i * 2 + d_half
                        at = i * RING + (g0 + RING)
                        beside(i, more, 0, 0)
                        pe.wait_ge(bank_free, at + 2)
                        scores(s + 1, 2, 3)
                        beside(i, more, 0, 1)
                        transposes(s, 0, maps)
                        beside(i, more, 1, 0)
                        pe.wait_ge(bank_free, at + 3)
                        pe.wait_ge(probT_done, s + 1)
                        heads(q, 0, cols[0])
                        beside(i, more, 1, 1)
                        if da:
                            head_statistic(d, 0)
                        transposes(s + 1, 1, maps)
                        beside(i, more, 2, 0)
                        pe.wait_ge(probT_done, s + 2)
                        heads(q + 1, 1, cols[1])
                        if more:
                            pe.wait_ge(bank_free, at + (RING + 1))
                            scores(s + 2, 0, 1)
                        beside(i, more, 2, 1)
                        if da:
                            head_statistic(d + 1, 1)

                    filled = {0: 5, 1: 6, 2: 6} if da else {}
                    if groups > 2:
                        with pe.Fori(0, groups - 1) as i:
                            group(i, True)
                    else:
                        group(0, True)
                    group(groups - 1, False)
                    half += 2 * groups
                    s_half += 2 * groups
                    if da:
                        d_half += 2 * groups
                    else:
                        k = n - 1
                        slot = slot_of(c0, k)
                        chunk_ready(c0 + k)
                        pe.wait_ge(pooled, POOL_STEPS)
                        for g in range(4):
                            bank = (pj[slot], tp[0])[g // 2]
                            done = product(bank[:, g % 2 * S:g % 2 * S + S], [w_tile(slot, g, P, 0)],
                                           [(act_hi[:, 16 + g, :], act_lo[:, 16 + g, :])])
                        done.then_inc(used, 1)
                    app += 1
                elif kind == "sb":
                    def sb_scores(b, slot):
                        bank = (sc, tp)[slot]
                        for m in range(2):
                            q = proj[64 * m:64 * m + 64, 2 * slot, :]
                            k = proj[64 * m:64 * m + 64, 2 * slot + 1, :]
                            pe.matmul(bank[m][:, 0:S], k[:, 0:QB], q, start=True, stop=False,
                                      skip_group_check=True)
                            done = pe.matmul(bank[m][:, S:CAUSAL], k[:, QB:S], q[:, QB:S], start=False,
                                             stop=False, skip_group_check=True)
                        done.then_inc(scores_done, 1)

                    def cumulate(b, slot):
                        pe.wait_ge(sp_masked, (b + slot) * 2 + 2)
                        bank = (sc, tp)[slot]
                        for m in range(2):
                            sp_ = prob[:, slot, m, :]
                            pe.matmul(bank[m][:, 0:S], neg_tri, sp_[:, 0:S], start=False, stop=False,
                                      skip_group_check=True)
                            pe.matmul(bank[m][:, QB:S], neg_ones, sp_[:, S:CAUSAL], start=False, stop=False,
                                      skip_group_check=True)
                            done = pe.matmul(bank[m][:, S:CAUSAL], neg_tri, sp_[:, S:CAUSAL], start=False,
                                             stop=True, skip_group_check=True)
                        done.then_inc(cum_done, 1)

                    filled = {0: 6, 1: 6, 2: 6}

                    def out_parts(at, k):
                        pe.wait_ge(mix_lo, half + filled[k])
                        for part in range(2):
                            out_part(at + k, slot_of(c0, k), part, 0, filled[k])

                    def group(i, more):
                        b, q = i * 2, i * 2 + half
                        at = i * RING + (c0 + RING)
                        if more:
                            project(at, slot_of(c0, 0))
                        else:
                            out_parts(at, 0)
                        cumulate(b, 0)
                        cumulate(b, 1)
                        if more:
                            project(at + 1, slot_of(c0, 1))
                        else:
                            out_parts(at, 1)
                        pe.wait_ge(bank_free, at + 3)
                        pe.wait_ge(a_masked, b * 2 + 2)
                        heads(q, 0, [0, 64])
                        if more:
                            project_v(at + 2, slot_of(c0, 2))
                        else:
                            out_parts(at, 2)
                        pe.wait_ge(a_masked, b * 2 + 4)
                        heads(q + 1, 1, [P, P + 64])
                        if more:
                            pe.wait_ge(bank_free, at + (RING + 2))
                            sb_scores(b + 2, 0)
                            sb_scores(b + 2, 1)

                    project(c0, slot_of(c0, 0), app)
                    project(c0 + 1, slot_of(c0, 1))
                    project_v(c0 + 2, slot_of(c0, 2))
                    pe.wait_ge(bank_free, RING + c0 + 2)
                    sb_scores(0, 0)
                    sb_scores(0, 1)
                    with pe.Fori(0, 3) as i:
                        group(i, True)
                    group(3, False)
                    half += 8
                    app += 1
                elif kind == "sw":
                    def v_at(j):
                        return P * (j // 4)

                    def kv(c, part, first=None):
                        slot = c % RING
                        if part == 0:
                            chunk_ready(c)
                            outputs(slot, 0, pj[slot][:, 0:S], first)
                        else:
                            project_tokens(slot, S, P, P)

                    kv(c0, 0, app)
                    kv(c0, 1)
                    project(c0 + 1, slot_of(c0, 1))
                    project_half(c0 + 2, slot_of(c0, 2), 0)
                    pe.wait_ge(bank_free, RING + c0 + 2)
                    scores(s_half, 0, 4)
                    project_half(c0 + 2, slot_of(c0, 2), 1)
                    scores(s_half + 1, 1, 4)
                    outs = {3: (0, 0, 3), 4: (1, 0, 4), 5: (2, 0, 5), 6: (0, 3, 6), 7: (1, 4, 6)}
                    filled = {0: 6, 1: 6, 2: 5}

                    def beside(j, part):
                        if j == 0:
                            kv(c0 + 3, part)
                        elif j < 3:
                            project_half(c0 + 3 + j, slot_of(c0, j), part)
                        else:
                            k, a, b = outs[j]
                            pe.wait_ge(mix_lo, half + b)
                            out_part(c0 + n + k, slot_of(c0, k), part, a, b)

                    for j in range(8):
                        q, s = half + j, s_half + j
                        transposes(s, j % 2, 2)
                        if j < 3:
                            beside(j, 0)
                        if j < 6:
                            pe.wait_ge(bank_free, RING + c0 + (3, 3, 5, 5, 6, 6)[j])
                            scores(s + 2, (j + 2) % 4, 4 if j < 2 else None)
                        if j >= 3:
                            beside(j, 0)
                        pe.wait_ge(probT_done, s + 1)
                        heads(q, j % 2, [v_at(j), v_at(j) + 64])
                        beside(j, 1)
                    half += 8
                    s_half += 8
                    app += 1
                elif kind == "wo":
                    for k in range(4):
                        slot = slot_of(c0, k)
                        a = filled.get(k, 0)
                        if a == 0:
                            chunk_ready(c0 + k)
                        if k == 0:
                            pe.wait_ge(mix_lo, half)
                            if layer == 4:
                                pe.wait_ge(bank_free, RING + c0)
                        for t in range(2):
                            out_part(c0 + k, slot, t, a, DT)
                    stat_of(f"wo{layer}")
                    if layer == 4:
                        stat_of("res_a")
                elif kind == "up":
                    def up(c, slot, first):
                        chunk_ready(c)
                        outputs(slot, 0, pj[slot][:, 0:S], first)
                        outputs(slot, 1, val_bank[slot][:, 0:S]).then_inc(used, 1)

                    up(c0, slot_of(c0, 0), app)
                    with pe.Fori(0, (n - 1) // RING) as i:
                        for k in range(RING):
                            up(i * RING + (c0 + 1 + k), slot_of(c0, 1 + k), None)
                    app += 1
                elif kind == "down":
                    def down(c, slot):
                        chunk_ready(c)
                        for k in range(FT):
                            if k == 0 or k >= FT - 3:
                                upto = FT - 3 if k == 0 else k + 1
                                pe.wait_ge(act_free, RING + ffn * FT + upto)
                            done = product(pj[slot][:, 0:S], [w_tile(slot, k, P, 0)],
                                           [(act_hi[:, k, :], act_lo[:, k, :])],
                                           start=k == 0, stop=k == FT - 1)
                        done.then_inc(used, 1)

                    with pe.Fori(0, 2) as i:
                        for k in range(RING):
                            down(i * RING + (c0 + k), slot_of(c0, k))
                    for k in range(2 * RING, DT):
                        down(c0 + k, slot_of(c0, k))
                    stat_of(f"down{layer}")
                    if layer == 3:
                        stat_of("final")
                    ffn += 1
                    layer += 1
                else:
                    pe.wait_ge(p_lo, 1)
                    for k in range(n):
                        slot = slot_of(c0, k)
                        chunk_ready(c0 + k)
                        for t in range(2):
                            product(val_bank[k % 3][:, t * S:t * S + S],
                                    [w_tile(slot, DT + f, 2 * P, t * P) for f in range(2)],
                                    [(act_hi[:, f, :], act_lo[:, f, :]) for f in range(2)])
                        outputs(slot, 0, pj[slot][:, 0:S], app if k == 0 else None)
                        outputs(slot, 1, pj[slot][:, S:2 * S]).then_inc(used, 1)


def _rows(w):
    return w.reshape(-1, P, w.shape[-1]).transpose(1, 0, 2)


def _chunk(*columns):
    return _rows(np.concatenate(columns, axis=1)).reshape(P, -1)


def _vector(v):
    return v.reshape(-1, P).T


def _heads(w, heads):
    return np.concatenate([w[:, 64 * h:64 * h + 64] for h in heads], axis=1)


def _buckets():
    dist = np.arange(NVEC) - 127
    d = np.maximum(dist, 0)
    large = 16 + (np.log(np.maximum(d, 1).astype(np.float32) / np.float32(16))
                  / np.float32(np.log(128 / 16)) * np.float32(16)).astype(np.int32)
    bucket = np.where(d < 16, d, np.minimum(large, 31))
    return dist, np.where(dist < 0, 32, bucket)


def kernel(**inputs):
    import concourse.bacc as bacc
    from concourse.bass_utils import run_bass_kernel_spmd as run

    a = {k: np.asarray(v) for k, v in inputs.items()}
    FF = a["ffn_w_down"].shape[1]

    std, down = [], []

    def grouped(w, first, groups, k_at, v_at):
        for i in range(groups):
            for t in (2 * i, 2 * i + 1):
                std.append(_chunk(w[:, first + P * t:first + P * t + P], w[:, k_at + P * t:k_at + P * t + P]))
            std.append(_chunk(w[:, v_at + 2 * P * i:v_at + 2 * P * i + 2 * P]))

    def pairs(w):
        for k in range(4):
            std.append(_chunk(w[:, 2 * P * k:2 * P * k + 2 * P]))

    def ffn(up, dn, width):
        pad = FT * P - width
        gate, val = (np.pad(up[:, g * width:(g + 1) * width], ((0, 0), (0, pad))) for g in range(2))
        for j in range(FT):
            std.append(_chunk(gate[:, P * j:P * j + P], val[:, P * j:P * j + P]))
        dn = np.pad(dn, ((0, pad), (0, 0)))
        for f in range(DT):
            down.append(_chunk(dn[:, P * f:P * f + P]))

    sw_tiles = [(8 * t + j, 8 * t + 4 + j) for t in range(2) for j in range(4)]
    for layer in range(4):
        w_o = a["w_o"][layer]
        if layer % 3 == 0:
            grouped(a["da_w_qkv"][layer // 3], 0, 4, D, 2 * D)
        elif layer == 1:
            grouped(a["sb_w_qkv"][0], 0, 4, D, 2 * D)
        else:
            w = a["sw_w_qkv"][0]
            for t in range(2):
                std.append(_chunk(w[:, D + P * t:D + P * t + P], w[:, D + 256 + P * t:D + 256 + P * t + P]))
                for j in (0, 2):
                    std.append(_chunk(*[_heads(w, sw_tiles[4 * t + j + e]) for e in range(2)]))
            w_o = np.concatenate([w_o[64 * h:64 * h + 64] for pair in sw_tiles for h in pair])
        pairs(w_o)
        ffn(a["ffn_w_up"][layer], a["ffn_w_down"][layer], FF)
    w_in = a["w_in_2"][0]
    for k in range(2):
        std.append(_chunk(w_in[:, 2 * P * k:2 * P * k + 2 * P]))
    grouped(w_in, 512, 2, 1024, 1536)
    std.append(np.pad(a["w_pool_2"][0].transpose(1, 0, 2).reshape(P, 4 * P), ((0, 0), (0, STD - 4 * P))))
    pairs(a["w_out_2"][0])
    ffn(a["w_up_2"][0], a["w_down_2"][0], a["w_down_2"].shape[1])
    gate = [np.concatenate([_chunk(a[w][0][:, 2 * P * k:2 * P * k + 2 * P]) for w in ("w_ple_gate_2", "w_ple_2")],
                           axis=1) for k in range(4)]

    par = np.zeros((P, NPAR), np.float32)

    def put(name, value, k=0):
        par[:, PARAM[name] + k:PARAM[name] + k + value.shape[1]] = value

    for layer in range(4):
        put("attn_norm", _vector(a["attn_norm"][layer]), DT * layer)
        put("ffn_norm", _vector(a["ffn_norm"][layer]), DT * layer)
        taps = np.concatenate([a["ffn_conv_w"][layer], a["ffn_conv_b"][layer][None]])
        taps = np.pad(taps.reshape(4, 2, FF), ((0, 0), (0, 0), (0, FT * P - FF)))
        put("conv", taps.reshape(4, 2, FT, P).transpose(3, 2, 1, 0).reshape(P, -1), FT * 8 * layer)
    for name, source in (("mix_pre", "g_mix_pre_2"), ("mix_post", "g_mix_post_2"),
                         ("ffn_pre", "g_ffn_pre_2"), ("ffn_post", "g_ffn_post_2")):
        put(name, _vector(a[source][0]))
    put("final_norm", _vector(a["final_norm"]))
    taps = np.concatenate([a["conv_w_2"][0], a["conv_b_2"][0][None]])
    put("conv2", taps.reshape(4, FT, P).transpose(2, 1, 0).reshape(P, -1))
    put("subln", a["da_subln"].T)
    sinks = a["sw_sinks"][0][np.array(sw_tiles)]
    put("sinks", np.broadcast_to(np.repeat(sinks, 2, axis=1).reshape(1, -1), (P, 32)))
    put("pool_scale", _vector(a["pool_scale_2"][0]))
    counts = [1.0 / min(t + 1, w) for w in WINDOWS for t in range(16)]
    put("inv_count", np.broadcast_to(np.array(counts, np.float32), (P, 64)))

    rows = np.arange(P)
    consts = np.concatenate([np.eye(P), np.ones((P, P)), -(rows[:, None] >= rows[None, :]).astype(np.float32),
                             -np.ones((P, P))], axis=1).astype(np.float32)
    dist, bucket = _buckets()
    onehot = (bucket[None, :] == np.arange(33)[:, None]).astype(np.float32)
    windowed = np.where(dist >= 128, 32, bucket)
    onehot_w = (windowed[None, :] == np.arange(33)[:, None]).astype(np.float32)
    rel, rel2 = a["rel_bias"], a["rel_bias_2"]
    tables = np.full((33, 48), NEG, np.float32)
    tables[0:32, 0:16] = rel
    tables[0:32, 16:32] = rel[:, np.array(sw_tiles).reshape(-1)]
    tables[0:32, 32:40] = rel2
    tables[:, 40:48] = 0.0

    arrays = {
        "xT": _rows(a["x"][0].T), "w_std": np.stack(std), "w_down": np.stack(down), "w_gate": np.stack(gate),
        "params": par, "consts": consts, "lam": np.broadcast_to(a["da_lambda"].reshape(1, 2, 256), (P, 2, 256)),
        "onehot": np.stack([onehot, onehot_w]), "tables": tables, "pT": _rows(a["p_2"][0, 0].T),
    }
    arrays = {k: np.ascontiguousarray(v) for k, v in arrays.items()}
    nc = bacc.Bacc("TRN2", target_bir_lowering=False, num_devices=1)
    args = [nc.dram_tensor(k, v.shape, mybir.dt.from_np(v.dtype), kind="ExternalInput").ap()
            for k, v in arrays.items()]
    out = nc.dram_tensor("out", (P, DT, S), F32, kind="ExternalOutput").ap()
    build(nc, *args, out)
    got = run(nc, [arrays], core_ids=[0]).results[0]["out"]
    return np.ascontiguousarray(got.transpose(1, 0, 2).reshape(D, S).T)[None]
```

```python
from contextlib import ExitStack

import numpy as np

import concourse.bass as bass
import concourse.mybir as mybir
from concourse.alu_op_type import AluOpType as ALU

F32 = mybir.dt.float32
F32R = mybir.dt.float32r
ACT = mybir.ActivationFunctionType

P = 128
S = 256
QB = 128
D = 1024
DT = D // P
FT = 22
RING = 3
STD = DT * 2 * P
DOWN = FT * P
GATE = STD + 2 * 2 * P
NEG = -1e30
EPS = 1e-6
CAUSAL = QB + S
NVEC = 383

PARAM = {}
_n = 0
for _name, _width in (("attn_norm", 4 * DT), ("ffn_norm", 4 * DT), ("final_norm", DT),
                      ("mix_pre", DT), ("mix_post", DT), ("ffn_pre", DT), ("ffn_post", DT),
                      ("conv", 4 * FT * 8), ("conv2", FT * 4), ("subln", 2), ("sinks", 8 * 4),
                      ("pool_scale", 4), ("inv_count", 4 * 16)):
    PARAM[_name] = _n
    _n += _width
NPAR = _n

STAGES = []
SIZES = []
for _kind, _count, _width in (
        ("da", 12, STD), ("wo", 4, STD), ("up", FT, STD), ("down", DT, DOWN),
        ("sb", 12, STD), ("wo", 4, STD), ("up", FT, STD), ("down", DT, DOWN),
        ("sw", 6, STD), ("wo", 4, STD), ("up", FT, STD), ("down", DT, DOWN),
        ("da", 12, STD), ("wo", 4, STD), ("up", FT, STD), ("down", DT, DOWN),
        ("mix", 9, STD), ("wo", 4, STD), ("up", FT, STD), ("down", DT, DOWN),
        ("gate", 4, GATE)):
    STAGES.append((_kind, len(SIZES), _count))
    SIZES += [_width] * _count
CHUNKS = len(SIZES)
EXP_AND_LN = 6
WINDOWS = (2, 4, 8, 16)
POOL_STEPS = sum(w.bit_length() - 1 + 4 for w in WINDOWS)


def lambda_init(layer):
    return 0.8 - 0.6 * float(np.exp(-0.3 * layer))


def build(nc, xT, w_std, w_down, w_gate, params, consts, lam, onehot, tables, pT, out):
    ctx = ExitStack()
    with ctx:
        def sb(name, shape, dt=F32):
            return ctx.enter_context(nc.sbuf_tensor(name, shape, dt))

        def sem(name):
            return ctx.enter_context(nc.semaphore(name))

        w_raw = sb("w_raw", [P, RING, DOWN])
        w_hi = sb("w_hi", [P, RING, DOWN], F32R)
        w_lo = sb("w_lo", [P, RING, DOWN], F32R)
        x = sb("x", [P, DT, S])
        h_hi = sb("h_hi", [P, DT, S], F32R)
        h_lo = sb("h_lo", [P, DT, S], F32R)
        act_hi = sb("act_hi", [P, FT, S], F32R)
        act_lo = sb("act_lo", [P, FT, S], F32R)
        par = sb("par", [P, NPAR])
        cst = sb("cst", [P, 4 * P])
        ident, ones = cst[:, 0:P], cst[:, P:2 * P]
        neg_tri, neg_ones = cst[:, 2 * P:3 * P], cst[:, 3 * P:4 * P]
        proj = sb("proj", [P, 5, S])
        vtok = sb("vtok", [P, 2, S])
        tmp = sb("tmp", [P, 12, S])
        sq = sb("sq", [P, 2, 2 * S])
        acc = sb("acc", [P, 2 * S])
        rstd = sb("rstd", [P, S])
        small = sb("small", [P, 2, 5, 4])
        odd = sb("odd", [P, 8])
        wait_mark = sb("wait_mark", [P, 2])
        u_sb = sb("u_sb", [P, 4, S])

        prob = tmp[:, 0:6, :].rearrange("p a b -> p (a b)").rearrange("p (h m c) -> p h m c", h=2, m=2)
        probT = tmp[:, 6:12, :].rearrange("p a b -> p (a b)").rearrange("p (h m c) -> p h m c", h=2, m=2)
        cgate, cval = tmp[:, 0:3, :], tmp[:, 3:6, :]

        banks = [ctx.enter_context(nc.psum_tensor(f"bank{b}", [P, 2 * S], F32)) for b in range(8)]
        pj = banks[0:3]
        val_bank = banks[3:6]
        sc = banks[3:5]
        tp = banks[5:7]
        ov = banks[7]

        arrived = [sem(f"arrived{s}") for s in range(RING)]
        hi_ready = sem("hi_ready")
        lo_ready = sem("lo_ready")
        used = sem("used")
        bank_free = sem("bank_free")
        setup_in = sem("setup_in")
        x_in = [sem(f"x_in{a}") for a in range(2)]
        consts_in = sem("consts_in")
        lam_dots = sem("lam_dots")
        lam_exp = sem("lam_exp")
        tile6_done = sem("tile6_done")
        x_part = sem("x_part")
        chain_a = sem("chain_a")
        sq_ready = sem("sq_ready")
        acc_done = sem("acc_done")
        x_ready = sem("x_ready")
        stat_done = sem("stat_done")
        rstd_done = sem("rstd_done")
        hf_done = sem("hf_done")
        h_hi_done = sem("h_hi_done")
        h_lo_even = sem("h_lo_even")
        h_lo_odd = sem("h_lo_odd")
        conv_init = sem("conv_init")
        conv_part = sem("conv_part")
        gated = sem("gated")
        prod_done = sem("prod_done")
        act_hi_done = sem("act_hi_done")
        act_free = sem("act_free")
        bias_in = [sem(f"bias_in{b}") for b in range(2)]
        scores_done = sem("scores_done")
        scores_taken = sem("scores_taken")
        dve_step = sem("dve_step")
        nmax_ready = sem("nmax_ready")
        sink_shift = sem("sink_shift")
        exp_done = sem("exp_done")
        probs_done = sem("probs_done")
        trans_done = sem("trans_done")
        probT_done = sem("probT_done")
        pv_done = sem("pv_done")
        head_out = sem("head_out")
        head_sq = sem("head_sq")
        head_stat = sem("head_stat")
        head_rstd = sem("head_rstd")
        head_norm = sem("head_norm")
        mix_hi = sem("mix_hi")
        mix_lo = sem("mix_lo")
        log_done = sem("log_done")
        sp_done = sem("sp_done")
        sp_masked = sem("sp_masked")
        cum_done = sem("cum_done")
        a_exp = sem("a_exp")
        a_masked = sem("a_masked")
        pool_hi = sem("pool_hi")
        pooled = sem("pooled")
        vec_psum = sem("vec_psum")
        vec_sb = sem("vec_sb")
        vec_out = sem("vec_out")
        tab_in = sem("tab_in")
        p_in = sem("p_in")
        p_hi = sem("p_hi")
        p_lo = sem("p_lo")
        sig_done = sem("sig_done")
        emb_done = sem("emb_done")
        out_ready = sem("out_ready")
        stored = sem("stored")

        vec_dram = nc.dram_tensor("vec_dram", (3, 16, NVEC), F32, kind="Internal")

        def param(name, k=0, width=1):
            at = PARAM[name] + k
            return par[:, bass.ds(at, width)] if not isinstance(at, int) else par[:, at:at + width]

        def slot_of(c0, k):
            return (c0 + k) % RING

        SUMS = {}
        added = parts = 0
        for name, singles in ([("x", False)]
                              + [(f"{k}{l}", k == "down") for l in range(4) for k in ("wo", "down")]
                              + [("final", False), ("wo4", False), ("res_a", False), ("down4", True)]):
            SUMS[name] = (added, parts, len(SUMS))
            added, parts = added + (7 if singles else 3), parts + (8 if singles else 5)

        def is_single(name):
            return name[0:4] == "down"

        def sum_part(name, j):
            if is_single(name):
                return (j, j + 1), (0, S), j % 2
            if j < 3:
                return (2 * j, 2 * j + 2), (0, 2 * S), j % 2
            return (j + 3, j + 4), ((j - 3) * S, (j - 2) * S), 1

        block = ctx.enter_context(nc.Block())

        @block.sync
        def _(sp):
            for n in range(2):
                a, b = n * DT // 2, (n + 1) * DT // 2
                sp.dma_start(x[:, a:b, :], xT[:, a:b, :]).then_inc(x_in[n], 16)
            sp.dma_start(cst[:, :], consts).then_inc(consts_in, 16)
            source = {STD: w_std, DOWN: w_down, GATE: w_gate}
            seen = {STD: 0, DOWN: 0, GATE: 0}

            def load(c, slot, width, row, wait=True):
                if wait:
                    sp.wait_ge(lo_ready, c - RING + 1)
                sp.dma_start(w_raw[:, slot, 0:width], source[width][row]).then_inc(arrived[slot], 16)

            c = 0
            while c < CHUNKS:
                width = SIZES[c]
                n = 1
                while c + n < CHUNKS and SIZES[c + n] == width:
                    n += 1
                row = seen[width]
                k = 0
                if c == 0:
                    for k in range(RING):
                        load(k, k, width, k, wait=False)
                        if k == 0:
                            sp.dma_start(par[:, :], params).then_inc(setup_in, 16)
                    k = RING
                turns = (n - k) // RING
                if turns > 1:
                    with sp.Fori(0, turns) as i:
                        for j in range(RING):
                            load(i * RING + (c + k + j), slot_of(c, k + j), width, i * RING + (row + k + j))
                    k += turns * RING
                while k < n:
                    load(c + k, slot_of(c, k), width, row + k)
                    k += 1
                seen[width] += n
                c += n
            for k in range(4):
                sp.wait_ge(out_ready, k + 1)
                sp.dma_start(out[:, 2 * k:2 * k + 2, :], x[:, 2 * k:2 * k + 2, :]).then_inc(stored, 16)
            sp.wait_ge(stored, 64)

        @block.scalar
        def _(act):
            def split_hi(c, slot, width, turn):
                act.wait_ge(arrived[slot], turn * 16 + 16)
                act.copy(w_hi[:, slot, 0:width], w_raw[:, slot, 0:width]).then_inc(hi_ready, 1)

            def next_split(c0, k, i=None):
                n = c0 + k + RING
                if i is None and n >= CHUNKS:
                    return
                shift = 0 if i is None else i * RING
                act.wait_ge(used, shift + (c0 + k + 1))
                turn = n // RING if i is None else i + n // RING
                split_hi(shift + n, n % RING, SIZES[n], turn)

            def squares(name, j, source=None):
                (a, b), (to, end), n = sum_part(name, j)
                busy = j - 1 if is_single(name) or j < 4 else 0
                if busy > 0:
                    act.wait_ge(acc_done, SUMS[name][0] + busy)
                if source is None:
                    source = x[:, a:b, :].rearrange("p a b -> p (a b)")
                act.activation(sq[:, n, to:end], source, ACT.Square).then_inc(sq_ready, 1)

            chained = [0]

            def chain(ins):
                chained[0] += 1
                ins.then_inc(chain_a, 1)
                act.wait_ge(chain_a, chained[0])

            def rms(norm):
                act.wait_ge(stat_done, norm + 1)
                chain(act.activation(rstd[:, :], ov[:, 0:S], ACT.Ln, bias=odd[:, 7:8], scale=1.0 / D))
                act.activation(rstd[:, :], rstd[:, :], ACT.Exp, scale=-0.5).then_inc(rstd_done, 1)

            def split_h(app):
                for k in range(DT):
                    act.wait_ge(hf_done, app * DT + k + 1)
                    act.copy(h_hi[:, k, :], tmp[:, k, :]).then_inc(h_hi_done, 1)

            def load_tables(functions):
                act.add_instruction(mybir.InstLoadActFuncSet(name=nc.get_next_instruction_name(),
                                                             act_func_set_id=functions))

            def exps(s_half, slot, sink):
                act.wait_ge(nmax_ready, s_half + 1)
                if sink:
                    act.wait_ge(sink_shift, sink)
                    act.activation(small[:, slot, 4, :], small[:, slot, 4, :], ACT.Exp)
                for m in range(2):
                    for qb, (a, b) in enumerate(((0, QB), (QB, CAUSAL))):
                        n = 2 * m + qb
                        last = act.activation(prob[:, slot, m, a:b], prob[:, slot, m, a:b], ACT.Exp,
                                              bias=small[:, slot, 1, n:n + 1],
                                              accum_out=small[:, slot, 2, n:n + 1])
                last.then_inc(exp_done, 1)

            def copy_probT(s_half, slot, maps):
                act.wait_ge(trans_done, s_half + 1)
                for m in range(maps):
                    last = act.copy(probT[:, slot, m, :], tp[m][:, 0:CAUSAL])
                last.then_inc(probT_done, 1)

            def mix_high(half, tile):
                act.wait_ge(pv_done, half + 1)
                act.copy(act_hi[:, tile, :], ov[:, 0:S]).then_inc(mix_hi, 1)

            def head_squares(half, d_half, slot):
                act.wait_ge(pv_done, half + 1)
                act.copy(u_sb[:, slot, :], ov[:, 0:S]).then_inc(head_out, 1)
                act.wait_ge(head_out, d_half + 1)
                act.activation(u_sb[:, 2 + slot, :], u_sb[:, slot, :], ACT.Square).then_inc(head_sq, 1)

            def head_rms(d_half, slot):
                act.wait_ge(head_stat, d_half + 1)
                act.activation(u_sb[:, 2 + slot, :], tp[1][:, 0:S], ACT.Ln, bias=odd[:, 7:8],
                               scale=1.0 / P).then_inc(head_rstd, 1)
                act.wait_ge(head_rstd, d_half * 2 + 1)
                act.activation(u_sb[:, 2 + slot, :], u_sb[:, 2 + slot, :], ACT.Exp, scale=-0.5)\
                   .then_inc(head_rstd, 1)

            def head_high(d_half, slot, tile):
                act.wait_ge(head_norm, d_half + 1)
                act.copy(act_hi[:, tile, :], u_sb[:, slot, :]).then_inc(mix_hi, 1)

            def evac_qk(c, slot, to):
                act.wait_ge(used, c + 1)
                act.mul(proj[:, 2 * to, :], pj[slot][:, 0:S], 0.125)
                act.copy(proj[:, 2 * to + 1, :], pj[slot][:, S:2 * S]).then_inc(bank_free, 1)

            def evac_v(c, slot, half):
                act.wait_ge(used, c + 1)
                if half is not None:
                    act.wait_ge(pv_done, half + 1)
                act.copy(vtok[:, :, :], pj[slot][:, :].rearrange("p (b f) -> p b f", b=2)).then_inc(bank_free, 1)

            load_tables(EXP_AND_LN)
            act.wait_ge(x_in[0], 16)
            squares("x", 0)
            squares("x", 1)
            act.wait_ge(x_in[1], 16)
            for j in range(2, 5):
                squares("x", j)
            split_hi(0, 0, SIZES[0], 0)
            postponed = []

            def postponed_splits():
                for c0_, k_ in postponed:
                    next_split(c0_, k_)
                postponed.clear()

            half = s_half = d_half = b_half = ffn = app = 0
            layer = 0
            prev = "x"
            for kind, c0, n in STAGES:
                if kind in ("da", "sb", "sw", "mix"):
                    groups = 2 if kind == "mix" else 4
                    rms(SUMS[prev][2])
                    split_h(app)
                    postponed_splits()
                    app += 1
                    if c0 == 0:
                        for c in (1, 2):
                            split_hi(c, c, SIZES[c], 0)
                        act.wait_ge(lam_dots, 4)
                        act.activation(odd[:, 0:4], odd[:, 0:4], ACT.Exp).then_inc(lam_exp, 1)
                    lead = 0
                    if kind == "mix":
                        for k in range(2):
                            act.wait_ge(used, c0 + k + 1)
                            act.copy(u_sb[:, 2 * k:2 * k + 2, :].rearrange("p a b -> p (a b)"),
                                     pj[slot_of(c0, k)][:, :]).then_inc(bank_free, 1)
                            next_split(c0, k)
                        lead = 2
                    g0 = c0 + lead

                    if kind in ("da", "mix"):
                        first_tile = 0 if kind == "da" else 4
                        maps = 1 if kind == "da" else 2
                        da = kind == "da"

                        def group(i, more):
                            q, s, d, t = (i * 2 + half, i * 2 + s_half, i * 2 + d_half, i * 2 + first_tile)
                            at = i * RING + (g0 + RING)
                            reg = i if not isinstance(i, int) else None
                            off = g0 + RING + (i * RING if isinstance(i, int) else 0)
                            exps(s + 1, 1, 0)
                            if more:
                                evac_qk(at, slot_of(g0, 0), 0)
                            copy_probT(s, 0, maps)
                            if not more and not da:
                                act.wait_ge(used, at + 1)
                                for g in range(4):
                                    bank = pj[slot_of(g0, g // 2 * 2)]
                                    act.mul(act_hi[:, g, :], bank[:, g % 2 * S:g % 2 * S + S],
                                            param("pool_scale", g)).then_inc(pool_hi, 1)
                                next_split(at, 0)
                            head_squares(q, d, 0) if da else mix_high(q, t)
                            if more:
                                next_split(off, 0, reg)
                            if da:
                                head_rms(d, 0)
                            if more:
                                evac_qk(at + 1, slot_of(g0, 1), 1)
                            copy_probT(s + 1, 1, maps)
                            if da:
                                head_high(d, 0, t)
                            if more:
                                next_split(off, 1, reg)
                            head_squares(q + 1, d + 1, 1) if da else mix_high(q + 1, t + 1)
                            if more:
                                exps(s + 2, 0, 0)
                                evac_v(at + 2, slot_of(g0, 2), q + 1)
                            if da:
                                head_rms(d + 1, 1)
                            if more:
                                next_split(off, 2, reg)
                            if da:
                                head_high(d + 1, 1, t + 1)

                        evac_qk(g0, slot_of(g0, 0), 0)
                        next_split(g0, 0)
                        evac_qk(g0 + 1, slot_of(g0, 1), 1)
                        next_split(g0, 1)
                        exps(s_half, 0, 0)
                        evac_v(g0 + 2, slot_of(g0, 2), None)
                        next_split(g0, 2)
                        if groups > 2:
                            with act.Fori(0, groups - 1) as i:
                                group(i, True)
                        else:
                            group(0, True)
                        group(groups - 1, False)
                        half += 2 * groups
                        s_half += 2 * groups
                        if kind == "da":
                            d_half += 2 * groups
                    elif kind == "sb":
                        def logs(b, slot):
                            act.wait_ge(scores_done, b + (half + slot + 1))
                            for m in range(2):
                                act.activation(prob[:, slot, m, :], (sc, tp)[slot][m][:, 0:CAUSAL], ACT.Abs)\
                                   .then_inc(log_done, 1)
                            for m in range(2):
                                act.wait_ge(log_done, (b + slot) * 6 + m + 1)
                                act.activation(prob[:, slot, m, :], prob[:, slot, m, :], ACT.Exp, scale=-1.0)\
                                   .then_inc(log_done, 1)
                            for m in range(2):
                                act.wait_ge(log_done, (b + slot) * 6 + m + 3)
                                act.activation(prob[:, slot, m, :], prob[:, slot, m, :], ACT.Ln, bias=1.0)\
                                   .then_inc(log_done, 1)

                        def a_exps(b, slot):
                            act.wait_ge(cum_done, b + slot + 1)
                            bank = (sc, tp)[slot]
                            for m in range(2):
                                act.activation(probT[:, slot, m, :], bank[m][:, 0:CAUSAL], ACT.Exp)\
                                   .then_inc(a_exp, 1)

                        def group(i, more):
                            b, q = i * 2, i * 2 + half
                            at = i * RING + (g0 + RING)
                            reg = i if not isinstance(i, int) else None
                            off = g0 + RING + (i * RING if isinstance(i, int) else 0)
                            logs(b, 0)
                            logs(b, 1)
                            if more:
                                evac_qk(at, slot_of(g0, 0), 0)
                            a_exps(b, 0)
                            if more:
                                next_split(off, 0, reg)
                            a_exps(b, 1)
                            if more:
                                evac_qk(at + 1, slot_of(g0, 1), 1)
                            mix_high(q, i * 2)
                            if more:
                                next_split(off, 1, reg)
                            mix_high(q + 1, i * 2 + 1)
                            if more:
                                evac_v(at + 2, slot_of(g0, 2), q + 1)
                                next_split(off, 2, reg)

                        evac_qk(g0, slot_of(g0, 0), 0)
                        next_split(g0, 0)
                        evac_qk(g0 + 1, slot_of(g0, 1), 1)
                        next_split(g0, 1)
                        evac_v(g0 + 2, slot_of(g0, 2), None)
                        next_split(g0, 2)
                        with act.Fori(0, groups - 1) as i:
                            group(i, True)
                        group(groups - 1, False)
                        half += 2 * groups
                    else:
                        def evac_kv(t):
                            act.wait_ge(used, c0 + 3 * t + 1)
                            bank = pj[slot_of(c0, 0)]
                            act.copy((proj[:, 4, :], u_sb[:, 0, :])[t], bank[:, 0:S])
                            act.copy(vtok[:, :, P * t:P * t + P],
                                     bank[:, S:2 * S].rearrange("p (b f) -> p b f", b=2)).then_inc(bank_free, 1)

                        def evac_q(c, pair):
                            act.wait_ge(used, c + 1)
                            act.mul(proj[:, 2 * pair:2 * pair + 2, :].rearrange("p a b -> p (a b)"),
                                    pj[c % RING][:, :], 0.125).then_inc(bank_free, 1)

                        evac_kv(0)
                        next_split(c0, 0)
                        evac_q(c0 + 1, 0)
                        exps(s_half, 0, 1)
                        next_split(c0, 1)
                        evac_q(c0 + 2, 1)
                        exps(s_half + 1, 1, 2)
                        next_split(c0, 2)
                        for j in range(8):
                            q, s = half + j, s_half + j
                            copy_probT(s, j % 2, 2)
                            if j == 0:
                                evac_kv(1)
                            elif j < 3:
                                evac_q(c0 + 3 + j, j - 1)
                            if j < 6:
                                exps(s + 2, j % 2, j + 3)
                            mix_high(q, j)
                            if j < 3:
                                next_split(c0 + 3, j)
                        half += 8
                        s_half += 8
                elif kind == "wo":
                    name = f"wo{layer}"
                    last_bank = val_bank[slot_of(c0, 3)]

                    def squared(k):
                        if layer < 4:
                            if k == 3:
                                act.wait_ge(x_part, layer + 1)
                            else:
                                act.wait_ge(bank_free, RING + c0 + min(k, 3) + 1)
                            squares(name, k)
                            return
                        if k == 3:
                            act.wait_ge(tile6_done, layer + 1)
                        else:
                            act.wait_ge(used, c0 + min(k, 3) + 1)
                        (a, b), _, _ = sum_part(name, k)
                        source = (last_bank[:, 0:S] if k == 4 else
                                  pj[slot_of(c0, k)][:, 0:(b - a) * S])
                        squares(name, k, source)
                        done = act.copy(tmp[:, a:b, :].rearrange("p a b -> p (a b)"), source)
                        if k != 3:
                            done.then_inc(bank_free, 1)

                    next_split(c0, 0)
                    squared(0)
                    squared(1)
                    next_split(c0, 1)
                    squared(2)
                    next_split(c0, 2)
                    squared(3)
                    squared(4)
                    rms(SUMS[name][2])
                    if layer == 4:
                        next_split(c0, 3)
                        for j in range(5):
                            act.wait_ge(x_ready, DT + (2 * j + 2 if j < 3 else j + 4))
                            squares("res_a", j)
                        rms(SUMS["res_a"][2])
                        split_h(app)
                    else:
                        split_h(app)
                        next_split(c0, 3)
                    app += 1
                elif kind == "up":
                    convs = 2 if ffn < 4 else 1

                    def step(j, c, slot, split):
                        n_ = j + ffn * FT
                        act.wait_ge(used, c + 1)
                        act.wait_ge(act_free, n_ + 1)
                        for v in range(convs):
                            bank, to = ((pj, cgate), (val_bank, cval))[v]
                            at = j * 8 + (4 * v + PARAM["conv"] + ffn * FT * 8) if ffn < 4 else j * 4 + PARAM["conv2"]
                            def col(k_):
                                return par[:, bass.ds(at + k_, 1)]
                            act.activation(to[:, slot, :], bank[slot][:, 0:S], ACT.Identity,
                                           bias=col(3), scale=col(2)).then_inc(conv_init, 1)
                        split()
                        act.wait_ge(conv_part, (j * 3 + (ffn * FT * 3 + 3)) if ffn < 4 else (j * 2 + (4 * FT * 3 + 2)))
                        act.activation(cgate[:, slot, :], cgate[:, slot, :],
                                       ACT.Silu if ffn < 4 else ACT.Gelu_apprx_tanh).then_inc(gated, 1)

                    turns = (n - RING) // RING
                    with act.Fori(0, turns) as i:
                        for k in range(RING):
                            step(i * RING + k, i * RING + (c0 + k), slot_of(c0, k),
                                 lambda: next_split(c0, k, i))
                    for j in range(turns * RING, n):
                        step(j, c0 + j, slot_of(c0, j), lambda: next_split(c0, j))
                    ffn += 1
                elif kind == "down":
                    load_tables(EXP_AND_LN)
                    name = f"down{layer}"
                    for k in range(DT):
                        if layer < 4:
                            act.wait_ge(bank_free, RING + c0 + k + 1)
                            squares(name, k)
                        else:
                            act.wait_ge(used, c0 + k + 1)
                            squares(name, k, pj[slot_of(c0, k)][:, 0:S])
                            act.copy(tmp[:, k, :], pj[slot_of(c0, k)][:, 0:S]).then_inc(bank_free, 1)
                        if k < DT - 1:
                            next_split(c0, k)
                    if layer == 3:
                        rms(SUMS[name][2])
                        next_split(c0, DT - 1)
                        for j in range(5):
                            act.wait_ge(x_ready, 2 * j + 2 if j < 3 else j + 4)
                            squares("final", j)
                        prev = "final"
                    elif layer == 4:
                        act.wait_ge(p_in, 16)
                        act.copy(act_hi[:, 0:2, :], u_sb[:, 0:2, :]).then_inc(p_hi, 1)
                        rms(SUMS[name][2])
                        for k in range(DT):
                            act.wait_ge(hf_done, app * DT + k + 1)
                            act.copy(h_hi[:, k, :], x[:, k, :]).then_inc(h_hi_done, 1)
                        next_split(c0, DT - 1)
                    else:
                        prev = name
                        postponed.append((c0, DT - 1))
                    layer += 1
                else:
                    for k in range(n):
                        act.wait_ge(used, c0 + k + 1)
                        act.activation(tmp[:, 2 * k:2 * k + 2, :].rearrange("p a b -> p (a b)"),
                                       pj[slot_of(c0, k)][:, :], ACT.Sigmoid).then_inc(sig_done, 1)
                        next_split(c0, k)

        @block.vector
        def _(dve):
            steps = [0]

            def wait_step():
                dve.wait_ge(dve_step, steps[0])

            def split_lo(c, slot, width):
                dve.wait_ge(hi_ready, c + 1)
                dve.tensor_tensor(w_lo[:, slot, 0:width], w_raw[:, slot, 0:width],
                                  w_hi[:, slot, 0:width].bitcast(F32), ALU.subtract).then_inc(lo_ready, 1)

            def next_split(c0, k, i=None):
                n = c0 + k + RING
                if i is None and n >= CHUNKS:
                    return
                split_lo(n if i is None else i * RING + n, n % RING, SIZES[n])

            def add_squares(name, j):
                _, (_, width), n = sum_part(name, j)
                a = j % 2 * S if is_single(name) else 0
                dve.wait_ge(sq_ready, SUMS[name][1] + j + 1)
                if SUMS[name][0] + j:
                    dve.wait_ge(acc_done, SUMS[name][0] + j)
                if j < (2 if is_single(name) else 1):
                    ins = dve.tensor_copy(acc[:, a:a + width], sq[:, n, 0:width])
                else:
                    ins = dve.tensor_tensor(acc[:, a:a + width], acc[:, a:a + width], sq[:, n, 0:width], ALU.add)
                ins.then_inc(acc_done, 1)

            def normalise(app, norm, gain):
                dve.wait_ge(rstd_done, norm + 1)

                def low(k):
                    dve.wait_ge(h_hi_done, app * DT + k + 1)
                    dve.tensor_tensor(h_lo[:, k, :], tmp[:, k, :], h_hi[:, k, :].bitcast(F32),
                                      ALU.subtract).then_inc(h_lo_even, 1)

                for k in range(DT):
                    dve.scalar_tensor_tensor(tmp[:, k, :], x[:, k, :], gain(k), rstd[:, :],
                                             ALU.mult, ALU.mult).then_inc(hf_done, 1)
                    if k % 2 and k > 1:
                        low(k - 3)
                low(DT - 2)

            def take_scores(half, s_half, turn, slot, sink):
                dve.wait_ge(scores_done, half + 1)
                dve.wait_ge(bias_in[slot], turn * 32 + 32)
                dve.memset(wait_mark[:, slot:slot + 1], 0.0)
                for m in range(2):
                    table = (act_hi, act_lo)[m]
                    for qb, (a, b, keys) in enumerate(((0, QB, QB), (QB, CAUSAL, S))):
                        n = 2 * m + qb
                        bias = table[:, 8 + slot, keys - 1::-1].bitcast(F32)
                        last = dve.tensor_tensor_reduce(prob[:, slot, m, a:b], sc[m][:, a:b],
                                                        bias, 1.0, NEG * 10,
                                                        ALU.add, ALU.max, small[:, slot, 0, n:n + 1])
                last.then_inc(scores_taken, 1)
                dve.wait_ge(scores_taken, s_half + 1)
                if sink is None:
                    dve.tensor_scalar(small[:, slot, 1, :], small[:, slot, 0, :], -1.0, None, ALU.mult)\
                       .then_inc(nmax_ready, 1)
                else:
                    col = param("sinks", 4 * sink, 4)
                    dve.tensor_tensor(small[:, slot, 0, :], small[:, slot, 0, :], col, ALU.max)\
                       .then_inc(dve_step, 1)
                    steps[0] += 1
                    wait_step()
                    dve.tensor_scalar(small[:, slot, 1, :], small[:, slot, 0, :], -1.0, None, ALU.mult)\
                       .then_inc(nmax_ready, 1)
                    dve.tensor_tensor(small[:, slot, 4, :], col, small[:, slot, 0, :], ALU.subtract)\
                       .then_inc(sink_shift, 1)

            def divide(s_half, slot, sink, base, lam_col=None):
                dve.wait_ge(exp_done, s_half + 1)
                done = 0

                def step(ins):
                    nonlocal done
                    done += 1
                    ins.then_inc(dve_step, 1)
                    dve.wait_ge(dve_step, base + done)

                if sink:
                    step(dve.tensor_tensor(small[:, slot, 2, :], small[:, slot, 2, :], small[:, slot, 4, :], ALU.add))
                step(dve.reciprocal(small[:, slot, 3, :], small[:, slot, 2, :]))
                spans = ((0, QB), (QB, CAUSAL))
                if lam_col is None:
                    for m in range(2):
                        for qb, (a, b) in enumerate(spans):
                            n = 2 * m + qb
                            last = dve.tensor_scalar(prob[:, slot, m, a:b], prob[:, slot, m, a:b],
                                                     small[:, slot, 3, n:n + 1], None, ALU.mult)
                else:
                    step(dve.tensor_scalar(small[:, slot, 4, 0:2], small[:, slot, 3, 2:4], lam_col, None, ALU.mult))
                    for qb, (a, b) in enumerate(spans):
                        ins = dve.tensor_scalar(prob[:, slot, 1, a:b], prob[:, slot, 1, a:b],
                                                small[:, slot, 4, qb:qb + 1], None, ALU.mult)
                    step(ins)
                    for qb, (a, b) in enumerate(spans):
                        last = dve.scalar_tensor_tensor(prob[:, slot, 0, a:b], prob[:, slot, 0, a:b],
                                                        small[:, slot, 3, qb:qb + 1], prob[:, slot, 1, a:b],
                                                        ALU.mult, ALU.add)
                last.then_inc(probs_done, 1)
                return done

            def add_normed(gain, signal, after=None):
                def scaled(k):
                    dve.scalar_tensor_tensor(tmp[:, k, :], tmp[:, k, :], param(gain, k),
                                             rstd[:, :], ALU.mult, ALU.mult).then_inc(dve_step, 1)
                    steps[0] += 1

                scaled(0)
                for k in range(DT):
                    if k + 1 < DT:
                        scaled(k + 1)
                    dve.wait_ge(dve_step, steps[0] - (1 if k + 1 < DT else 0))
                    dve.tensor_tensor(x[:, k, :], x[:, k, :], tmp[:, k, :], ALU.add).then_inc(signal, 1)
                    if after is not None:
                        after(k)

            def mix_low(half, tile):
                dve.wait_ge(mix_hi, half + 1)
                dve.tensor_tensor(act_lo[:, tile, :], ov[:, 0:S], act_hi[:, tile, :].bitcast(F32),
                                  ALU.subtract).then_inc(mix_lo, 1)

            def head_normed(d_half, slot, da_layer):
                dve.wait_ge(head_rstd, d_half * 2 + 2)
                dve.scalar_tensor_tensor(u_sb[:, slot, :], u_sb[:, slot, :], odd[:, 4 + da_layer:5 + da_layer],
                                         u_sb[:, 2 + slot, :], ALU.mult, ALU.mult).then_inc(head_norm, 1)

            def head_low(half, slot, tile):
                dve.wait_ge(mix_hi, half + 1)
                dve.tensor_tensor(act_lo[:, tile, :], u_sb[:, slot, :], act_hi[:, tile, :].bitcast(F32),
                                  ALU.subtract).then_inc(mix_lo, 1)

            for b, free in enumerate([bank_free] * RING + [act_free] * RING):
                dve.memset(small[:, b // 5, b % 5, :], 0.0).then_inc(free, 1)
            dve.memset(odd[:, 7:8], EPS).then_inc(dve_step, 1)
            steps[0] += 1
            wait_step()
            for j in range(3):
                add_squares("x", j)
            split_lo(0, 0, SIZES[0])

            def first_layer():
                for c in (1, 2):
                    split_lo(c, c, SIZES[c])
                dve.wait_ge(tab_in, 64)
                lam_sb = tmp[:, 8:10, :]
                for l in range(2):
                    for a in range(2):
                        dve.tensor_tensor_reduce(tmp[:, 11, 64 * (2 * l + a):64 * (2 * l + a) + 64],
                                                 lam_sb[:, l, 128 * a:128 * a + 64],
                                                 lam_sb[:, l, 128 * a + 64:128 * a + 128], 1.0, 0.0,
                                                 ALU.mult, ALU.add, odd[:, 2 * l + a:2 * l + a + 1])\
                           .then_inc(lam_dots, 1)
                for t in range(3):
                    dve.wait_ge(vec_psum, t + 1)
                    dve.tensor_copy((sq[0:16, 0, 0:NVEC], sq[0:16, 1, 0:NVEC], acc[0:16, 0:NVEC])[t],
                                    banks[3 + t][0:16, 0:NVEC]).then_inc(vec_sb, 1)
                dve.wait_ge(lam_exp, 1)
                for l in range(2):
                    dve.tensor_tensor(odd[:, 2 * l:2 * l + 1], odd[:, 2 * l + 1:2 * l + 2], odd[:, 2 * l:2 * l + 1],
                                      ALU.subtract).then_inc(dve_step, 1)
                    dve.tensor_scalar(odd[:, 4 + l:5 + l], param("subln", l), 1.0 - lambda_init(3 * l), None,
                                      ALU.mult).then_inc(dve_step, 1)
                    steps[0] += 2
                wait_step()
                for l in range(2):
                    dve.tensor_scalar(odd[:, 2 * l:2 * l + 1], odd[:, 2 * l:2 * l + 1], -lambda_init(3 * l), None,
                                      ALU.add).then_inc(dve_step, 1)
                    steps[0] += 1
                wait_step()

            postponed = []

            def postponed_splits():
                for c0_, k_ in postponed:
                    next_split(c0_, k_)
                postponed.clear()

            half = s_half = d_half = ffn = app = 0
            layer = 0
            da_layer = 0
            prev = "x"
            for kind, c0, n in STAGES:
                if kind in ("da", "sb", "sw", "mix"):
                    groups = 2 if kind == "mix" else 4
                    gain_name = "attn_norm" if kind != "mix" else "mix_pre"
                    if c0 == 0:
                        dve.wait_ge(setup_in, 16)
                    normalise(app, SUMS[prev][2],
                              lambda k: param(gain_name, k + (DT * layer if layer < 4 else 0)))
                    postponed_splits()
                    if c0 == 0:
                        first_layer()
                    app += 1
                    lead = 0
                    if kind == "mix":
                        for k in range(2):
                            next_split(c0, k)
                        lead = 2
                    g0 = c0 + lead
                    if kind in ("da", "mix"):
                        per = 3 if kind == "da" else 1
                        lam_col = odd[:, 2 * da_layer:2 * da_layer + 1] if kind == "da" else None
                        base = steps[0]

                        first_tile = 0 if kind == "da" else 4
                        da = kind == "da"

                        def group(i, more):
                            q, s, d, t = (i * 2 + half, i * 2 + s_half, i * 2 + d_half, i * 2 + first_tile)
                            b = i * (2 * per) + base
                            reg = i if not isinstance(i, int) else None
                            off = g0 + RING + (i * RING if isinstance(i, int) else 0)
                            take_scores(q + 1, s + 1, i + s_half // 2, 1, None)
                            divide(s + 1, 1, False, b + per, lam_col)
                            if more:
                                next_split(off, 0, reg)
                            if not more and not da:
                                dve.wait_ge(pool_hi, 4)
                                for g in range(4):
                                    bank = pj[slot_of(g0, g // 2 * 2)]
                                    last = dve.scalar_tensor_tensor(act_lo[:, g, :], bank[:, g % 2 * S:g % 2 * S + S],
                                                                    param("pool_scale", g),
                                                                    act_hi[:, g, :].bitcast(F32),
                                                                    ALU.mult, ALU.subtract)
                                last.then_inc(bank_free, 1)
                                next_split(off, 0)
                            if da:
                                head_normed(d, 0, da_layer)
                                head_low(q, 0, t)
                            else:
                                mix_low(q, t)
                            if more:
                                next_split(off, 1, reg)
                                take_scores(q + 2, s + 2, i + (s_half // 2 + 1), 0, None)
                                divide(s + 2, 0, False, b + 2 * per, lam_col)
                            if da:
                                head_normed(d + 1, 1, da_layer)
                            else:
                                mix_low(q + 1, t + 1)
                            if more:
                                next_split(off, 2, reg)
                            if da:
                                head_low(q + 1, 1, t + 1)

                        next_split(g0, 0)
                        next_split(g0, 1)
                        take_scores(half, s_half, s_half // 2, 0, None)
                        assert divide(s_half, 0, False, base, lam_col) == per
                        next_split(g0, 2)
                        if groups > 2:
                            with dve.Fori(0, groups - 1) as i:
                                group(i, True)
                        else:
                            group(0, True)
                        group(groups - 1, False)
                        steps[0] += 2 * per * groups
                        half += 2 * groups
                        s_half += 2 * groups
                        if kind == "da":
                            d_half += 2 * groups
                            da_layer += 1
                    elif kind == "sb":
                        def softplus(b, slot):
                            for m in range(2):
                                bank = (sc, tp)[slot]
                                dve.wait_ge(log_done, (b + slot) * 6 + m + 5)
                                dve.scalar_tensor_tensor(prob[:, slot, m, :], bank[m][:, 0:CAUSAL], 0.0,
                                                         prob[:, slot, m, :], ALU.max, ALU.add)\
                                   .then_inc(sp_done, 1)

                        def group(i, more):
                            b, q = i * 2, i * 2 + half
                            reg = i if not isinstance(i, int) else None
                            off = g0 + RING + (i * RING if isinstance(i, int) else 0)
                            softplus(b, 0)
                            softplus(b, 1)
                            if more:
                                next_split(off, 0, reg)
                                next_split(off, 1, reg)
                            mix_low(q, i * 2)
                            mix_low(q + 1, i * 2 + 1)
                            if more:
                                next_split(off, 2, reg)

                        for k in range(3):
                            next_split(g0, k)
                        with dve.Fori(0, groups - 1) as i:
                            group(i, True)
                        group(groups - 1, False)
                        half += 2 * groups
                    else:
                        def take(j):
                            take_scores(half + j, s_half + j, (s_half + j) // 2, j % 2, j)

                        next_split(c0, 0)
                        take(0)
                        next_split(c0, 1)
                        take(1)
                        steps[0] += divide(s_half, 0, True, steps[0])
                        next_split(c0, 2)
                        steps[0] += divide(s_half + 1, 1, True, steps[0])
                        for j in range(8):
                            if j < 6:
                                take(j + 2)
                            mix_low(half + j, j)
                            if j < 6:
                                steps[0] += divide(s_half + j + 2, j % 2, True, steps[0])
                            if j < 3:
                                next_split(c0 + 3, j)
                        half += 8
                        s_half += 8
                elif kind == "wo":
                    name = f"wo{layer}"

                    def added_to_x(k):
                        if layer == 4:
                            return
                        if k == 3:
                            dve.wait_ge(tile6_done, layer + 1)
                        else:
                            dve.wait_ge(used, c0 + min(k, 3) + 1)
                        (a, b), _, _ = sum_part(name, k)
                        xk = x[:, a:b, :].rearrange("p a b -> p (a b)")
                        bank = val_bank[slot_of(c0, 3)] if k == 4 else pj[slot_of(c0, k)]
                        dve.tensor_tensor(xk, bank[:, 0:(b - a) * S], xk, ALU.add)\
                           .then_inc(x_part if k == 3 else bank_free, 1)

                    added_to_x(0)
                    next_split(c0, 0)
                    added_to_x(1)
                    added_to_x(2)
                    add_squares(name, 0)
                    add_squares(name, 1)
                    next_split(c0, 1)
                    add_squares(name, 2)
                    next_split(c0, 2)
                    added_to_x(3)
                    added_to_x(4)
                    if layer < 4:
                        normalise(app, SUMS[name][2], lambda k: param("ffn_norm", k + DT * layer))
                        next_split(c0, 3)
                    else:
                        dve.wait_ge(rstd_done, SUMS[name][2] + 1)
                        add_normed("mix_post", x_ready)
                        for j in range(3):
                            add_squares("res_a", j)
                        next_split(c0, 3)
                        normalise(app, SUMS["res_a"][2], lambda k: param("ffn_pre", k))
                    app += 1
                elif kind == "up":
                    def step(j, c, slot, split):
                        n_ = j + ffn * FT
                        convs = 2 if ffn < 4 else 1
                        at = j * 8 + (PARAM["conv"] + ffn * FT * 8) if ffn < 4 else j * 4 + PARAM["conv2"]
                        init = j * 2 + ffn * FT * 2 if ffn < 4 else j + 4 * FT * 2
                        part = j * 3 + ffn * FT * 3 if ffn < 4 else j * 2 + 4 * FT * 3

                        def tap(v, lag):
                            bank, to = ((pj, cgate), (val_bank, cval))[v]
                            return dve.scalar_tensor_tensor(
                                to[:, slot, lag:S], bank[slot][:, 0:S - lag],
                                par[:, bass.ds(at + (4 * v + 2 - lag), 1)], to[:, slot, lag:S],
                                ALU.mult, ALU.add)

                        for v in range(convs):
                            dve.wait_ge(conv_init, init + (v + 1))
                            tap(v, 1).then_inc(conv_part, 1)
                        dve.wait_ge(conv_part, part + 1)
                        tap(0, 2).then_inc(conv_part, 1)
                        if convs == 2:
                            dve.wait_ge(conv_part, part + 2)
                            tap(1, 2).then_inc(bank_free, 1)
                        split()
                        dve.wait_ge(gated, n_ + 1)
                        if convs == 2:
                            dve.wait_ge(bank_free, c + (RING + 1))
                            dve.tensor_tensor(cval[:, slot, :], cgate[:, slot, :], cval[:, slot, :],
                                              ALU.mult).then_inc(prod_done, 1)
                        else:
                            dve.tensor_tensor(cval[:, slot, :], val_bank[slot][:, 0:S], cgate[:, slot, :],
                                              ALU.mult).then_inc(bank_free, 1)

                    turns = (n - RING) // RING
                    with dve.Fori(0, turns) as i:
                        for k in range(RING):
                            step(i * RING + k, i * RING + (c0 + k), slot_of(c0, k),
                                 lambda: next_split(c0, k, i))
                    for j in range(turns * RING, n):
                        step(j, c0 + j, slot_of(c0, j), lambda: next_split(c0, j))
                    ffn += 1
                elif kind == "down":
                    name = f"down{layer}"
                    for k in range(DT):
                        if layer < 4:
                            dve.wait_ge(used, c0 + k + 1)
                            dve.tensor_tensor(x[:, k, :], pj[slot_of(c0, k)][:, 0:S], x[:, k, :], ALU.add)\
                               .then_inc(bank_free, 1)
                        if k < DT - 1:
                            add_squares(name, k)
                            next_split(c0, k)
                    if layer == 3:
                        dve.wait_ge(rstd_done, SUMS[name][2] + 1)
                        for k in range(DT):
                            dve.scalar_tensor_tensor(x[:, k, :], x[:, k, :], param("final_norm", k),
                                                     rstd[:, :], ALU.mult, ALU.mult).then_inc(x_ready, 1)
                        for j in range(3):
                            add_squares("final", j)
                        next_split(c0, DT - 1)
                        prev = "final"
                    elif layer == 4:
                        dve.wait_ge(p_hi, 1)
                        dve.tensor_tensor(act_lo[:, 0:2, :], u_sb[:, 0:2, :], act_hi[:, 0:2, :].bitcast(F32),
                                          ALU.subtract).then_inc(p_lo, 1)
                        dve.wait_ge(rstd_done, SUMS[name][2] + 1)

                        def low(k):
                            if k % 2:
                                dve.wait_ge(h_hi_done, app * DT + k)
                                dve.tensor_tensor(h_lo[:, k - 1, :], x[:, k - 1, :],
                                                  h_hi[:, k - 1, :].bitcast(F32),
                                                  ALU.subtract).then_inc(h_lo_even, 1)

                        add_normed("ffn_post", hf_done, low)
                        next_split(c0, DT - 1)
                    else:
                        prev = name
                        postponed.append((c0, DT - 1))
                    layer += 1
                else:
                    for k in range(n):
                        next_split(c0, k)
                        both = tmp[:, 2 * k:2 * k + 2, :].rearrange("p a b -> p (a b)")
                        xk = x[:, 2 * k:2 * k + 2, :].rearrange("p a b -> p (a b)")
                        dve.wait_ge(sig_done, k + 1)
                        dve.tensor_tensor(both, val_bank[k % 3][:, :], both, ALU.mult).then_inc(bank_free, 1)
                        dve.wait_ge(bank_free, RING + c0 + k + 1)
                        dve.tensor_tensor(xk, xk, both, ALU.add).then_inc(out_ready, 1)

        @block.gpsimd
        def _(pool):
            def bias_dma(table, s, slot, pair, free=True):
                if free:
                    pool.wait_ge(scores_taken, s - 1)
                for m, to in enumerate((act_hi, act_lo)):
                    src = bass.AP(tensor=vec_dram, offset=pair * (2 * NVEC) + (table * 16 + m) * NVEC,
                                  ap=[[1, P], [1, S]])
                    pool.dma_start(to[:, 8 + slot, :].bitcast(F32), src).then_inc(bias_in[slot], 16)

            def low_odd(app, source):
                for k in range(1, DT, 2):
                    pool.wait_ge(h_hi_done, app * DT + k + 1)
                    pool.tensor_tensor(h_lo[:, k, :], source[:, k, :], h_hi[:, k, :].bitcast(F32),
                                       ALU.subtract).then_inc(h_lo_odd, 1)

            own = [0]

            def step(ins):
                own[0] += 1
                ins.then_inc(pooled, 1)
                pool.wait_ge(pooled, own[0])

            for t in range(2):
                pool.dma_start(u_sb[0:33, 2 * t:2 * t + 2, :].rearrange("p a b -> p (a b)")[:, 0:NVEC], onehot[t])\
                    .then_inc(tab_in, 16)
            pool.dma_start(tmp[0:33, 10, 0:48], tables).then_inc(tab_in, 16)
            pool.dma_start(tmp[:, 8:10, :], lam).then_inc(tab_in, 16)

            s_half = ffn = app = layer = 0
            for kind, c0, n in STAGES:
                if kind in ("da", "sw", "mix"):
                    table = {"da": 0, "sw": 1, "mix": 2}[kind]
                    halves = 4 if kind == "mix" else 8
                    if c0:
                        pool.wait_ge(used, c0)
                    if c0 == 0:
                        low_odd(app, tmp)
                        pool.wait_ge(vec_sb, 3)
                        for t, src in enumerate((sq[0:16, 0, 0:NVEC], sq[0:16, 1, 0:NVEC], acc[0:16, 0:NVEC])):
                            pool.dma_start(vec_dram[t], src).then_inc(vec_out, 16)
                        pool.wait_ge(vec_out, 48)
                    for b in range(2):
                        bias_dma(table, s_half + b, b, b, free=s_half > 0)
                    if c0:
                        low_odd(app, tmp)
                    app += 1
                    if kind == "mix":
                        pool.wait_ge(bank_free, RING + c0 + 2)
                        for g, w in enumerate(WINDOWS):
                            src, k, at = u_sb[:, g, :], 1, 0
                            while k < w:
                                dst = sq[:, 0, at * S:at * S + S]
                                pool.tensor_copy(dst[:, 0:k], src[:, 0:k])
                                step(pool.tensor_tensor(dst[:, k:S], src[:, k:S], src[:, 0:S - k], ALU.add))
                                src, k, at = dst, 2 * k, 1 - at
                            dst = sq[:, 1, 0:S]
                            pool.tensor_tensor(dst[:, 0:16], src[:, 0:16], param("inv_count", 16 * g, 16), ALU.mult)
                            step(pool.tensor_scalar(dst[:, 16:S], src[:, 16:S], 1.0 / w, None, ALU.mult))
                            mean = sq[:, 1, S:2 * S]
                            step(pool.tensor_tensor(mean, dst, u_sb[:, g, :], ALU.subtract))
                            step(pool.tensor_copy(act_hi[:, 16 + g, :], mean))
                            step(pool.tensor_tensor(act_lo[:, 16 + g, :], mean,
                                                    act_hi[:, 16 + g, :].bitcast(F32), ALU.subtract))
                    if kind == "da":
                        with pool.Fori(1, halves // 2) as i:
                            for b in range(2):
                                bias_dma(table, i * 2 + (s_half + b), b, i * 2 + b)
                    else:
                        for h in range(2, halves):
                            bias_dma(table, s_half + h, h % 2, h)
                    s_half += halves
                elif kind == "sb":
                    low_odd(app, tmp)
                    app += 1

                    def mask(buffer, slot, m):
                        v = buffer[:, slot, m, :].rearrange("p (b c) -> p b c", c=P)[:, 0:3:2, :]
                        return pool.affine_select(out=v, in_=v, compare_op=ALU.is_gt, fill=0.0, base=0,
                                                  pattern=[[0, 2], [1, P]], channel_multiplier=-1)

                    for i in range(4):
                        for slot in range(2):
                            for m in range(2):
                                pool.wait_ge(sp_done, i * 4 + (2 * slot + m + 1))
                                mask(prob, slot, m).then_inc(sp_masked, 1)
                        for slot in range(2):
                            for m in range(2):
                                pool.wait_ge(a_exp, i * 4 + (2 * slot + m + 1))
                                mask(probT, slot, m).then_inc(a_masked, 1)
                elif kind == "wo":
                    low_odd(app, tmp)
                    app += 1
                elif kind == "up":
                    def split_act(j, c, slot):
                        n_ = j + ffn * FT
                        if ffn < 4:
                            pool.wait_ge(prod_done, n_ + 1)
                        else:
                            pool.wait_ge(bank_free, c + (RING + 1))
                        pool.tensor_copy(act_hi[:, bass.ds(j, 1), :].squeeze(1) if not isinstance(j, int) else
                                         act_hi[:, j, :], cval[:, slot, :]).then_inc(act_hi_done, 1)
                        pool.wait_ge(act_hi_done, n_ + 1)
                        pool.tensor_tensor(act_lo[:, j, :], cval[:, slot, :], act_hi[:, j, :].bitcast(F32),
                                           ALU.subtract).then_inc(act_free, 1)

                    with pool.Fori(0, n // RING) as i:
                        for k in range(RING):
                            split_act(i * RING + k, i * RING + (c0 + k), slot_of(c0, k))
                    for j in range(n // RING * RING, n):
                        split_act(j, c0 + j, slot_of(c0, j))
                    ffn += 1
                elif kind == "down":
                    if layer == 4:
                        pool.dma_start(u_sb[:, 0:2, :], pT).then_inc(p_in, 16)
                        low_odd(app, x)
                    layer += 1

        @block.tensor
        def _(pe):
            def product(dst, weights, moving, start=True, stop=True, shared=False):
                for k, ((wh, wl), (xh, xl)) in enumerate(zip(weights, moving)):
                    first, last = start and k == 0, stop and k == len(weights) - 1
                    pe.matmul(dst, wh, xh, start=first, stop=False, skip_group_check=shared)
                    pe.matmul(dst, wh, xl, start=False, stop=False, skip_group_check=shared)
                    done = pe.matmul(dst, wl, xh, start=False, stop=last, skip_group_check=shared)
                return done

            def chunk_ready(c):
                pe.wait_ge(lo_ready, c + 1)
                pe.wait_ge(bank_free, c + 1)

            def w_tile(slot, k, width, at):
                a = k * width + at
                return w_hi[:, slot, a:a + P], w_lo[:, slot, a:a + P]

            def h_tile(k, a=0, b=S):
                return h_hi[:, k, a:b], h_lo[:, k, a:b]

            def outputs(slot, tile, dst):
                return product(dst, [w_tile(slot, k, 2 * P, tile * P) for k in range(DT)],
                               [h_tile(k) for k in range(DT)])

            def first_outputs(app, sums, shared=True):
                for k in range(DT):
                    pe.wait_ge(h_hi_done, app * DT + k + 1)
                    for n, (dst, operands) in enumerate(sums):
                        (wh, wl), (xh, xl), swap = operands(k)
                        for w in (wh, wl):
                            a, b = (xh, w) if swap else (w, xh)
                            pe.matmul(dst, a, b, start=k == 0 and w is wh and (n == 0 or not shared),
                                      stop=False, skip_group_check=shared)
                    pe.wait_ge(h_lo_odd if k % 2 else h_lo_even, app * (DT // 2) + k // 2 + 1)
                    for n, (dst, operands) in enumerate(sums):
                        (wh, wl), (xh, xl), swap = operands(k)
                        a, b = (xl, wh) if swap else (wh, xl)
                        done = pe.matmul(dst, a, b, start=False, stop=k == DT - 1, skip_group_check=shared)
                return done

            def pair(c, slot, dsts, app, shared=True):
                chunk_ready(c)
                first_outputs(app, [(dst, lambda k, t=t: (w_tile(slot, k, 2 * P, t * P), h_tile(k), False))
                                    for t, dst in enumerate(dsts)], shared).then_inc(used, 1)

            def project(c, slot, app=None):
                if app is not None:
                    pair(c, slot, (pj[slot][:, 0:S], pj[slot][:, S:2 * S]), app)
                    return
                chunk_ready(c)
                outputs(slot, 0, pj[slot][:, 0:S])
                outputs(slot, 1, pj[slot][:, S:2 * S]).then_inc(used, 1)

            def project_half(c, slot, tile):
                if tile == 0:
                    chunk_ready(c)
                done = outputs(slot, tile, pj[slot][:, tile * S:tile * S + S])
                if tile:
                    done.then_inc(used, 1)

            def out_part(c, slot, tile, a, b, dst=None, start=None):
                if start is None:
                    start = a == 0 and (tile == 0 or dst is not None)
                    if a == 0 and tile == 0:
                        chunk_ready(c)
                done = product(pj[slot][:, tile * S:tile * S + S] if dst is None else dst,
                               [w_tile(slot, f, 2 * P, tile * P) for f in range(a, b)],
                               [(act_hi[:, f, :], act_lo[:, f, :]) for f in range(a, b)],
                               start=start, stop=b == DT, shared=True)
                if tile and b == DT:
                    done.then_inc(used, 1)
                return done

            def project_tokens(slot, at, a, width, blocks=(0, 1)):
                for b in blocks:
                    done = product(pj[slot][:, at + b * width:at + (b + 1) * width],
                                   [h_tile(k, b * P, b * P + P) for k in range(DT)],
                                   [(w_hi[:, slot, k * S + a:k * S + a + width],
                                     w_lo[:, slot, k * S + a:k * S + a + width]) for k in range(DT)])
                if blocks[-1] == 1:
                    done.then_inc(used, 1)

            def project_v(c, slot):
                chunk_ready(c)
                project_tokens(slot, 0, 0, 2 * P)

            def statistic(name):
                singles = is_single(name)
                added, parts, _ = SUMS[name]
                pe.wait_ge(acc_done, added + (7 if singles else 3))
                pe.matmul(ov[:, 0:S], ones, acc[:, 0:S], start=True, stop=False)
                pe.matmul(ov[:, 0:S], ones, acc[:, S:2 * S], start=False, stop=False)
                for j in ((7,) if singles else (3, 4)):
                    _, (a, b), n = sum_part(name, j)
                    pe.wait_ge(sq_ready, parts + j + 1)
                    done = pe.matmul(ov[:, 0:S], ones, sq[:, n, a:b], start=False, stop=j in (7, 4))
                done.then_inc(stat_done, 1)

            def scores(s_half, q_tile, k_tile):
                pe.wait_ge(scores_taken, s_half)
                for m in range(2):
                    q = proj[64 * m:64 * m + 64, q_tile, :]
                    k = (u_sb[64 * m:64 * m + 64, 0, :] if k_tile is None else
                         proj[64 * m:64 * m + 64, k_tile, :])
                    pe.matmul(sc[m][:, 0:QB], q[:, 0:QB], k[:, 0:QB], start=True, stop=True)
                    done = pe.matmul(sc[m][:, QB:CAUSAL], q[:, QB:S], k, start=True, stop=True)
                done.then_inc(scores_done, 1)

            def transposes(s_half, slot, maps):
                pe.wait_ge(probs_done, s_half + 1)
                pe.wait_ge(probT_done, s_half)
                for m in range(maps):
                    for b in range(3):
                        done = pe.transpose(tp[m][:, b * P:b * P + P], prob[:, slot, m, b * P:b * P + P], ident)
                done.then_inc(trans_done, 1)

            def heads(half, slot, columns):
                pe.wait_ge(mix_lo, half)
                n = P // len(columns)
                for m, a in enumerate(columns):
                    to = ov[n * m:n * m + n, :]
                    pe.matmul(to[:, 0:S], vtok[:, 0, a:a + n], probT[:, slot, m, 0:S], start=True, stop=False)
                    done = pe.matmul(to[:, QB:S], vtok[:, 1, a:a + n], probT[:, slot, m, S:CAUSAL],
                                     start=False, stop=True)
                done.then_inc(pv_done, 1)

            def bias_vectors():
                pe.wait_ge(tab_in, 64)
                for t in range(3):
                    a = (0, 2, 0)[t]
                    pe.matmul(banks[3 + t][0:16, 0:NVEC], tmp[0:33, 10, 16 * t:16 * t + 16],
                              u_sb[0:33, a:a + 2, :].rearrange("p a b -> p (a b)")[:, 0:NVEC],
                              start=True, stop=True).then_inc(vec_psum, 1)

            pe.wait_ge(consts_in, 16)
            statistic("x")

            half = s_half = d_half = ffn = app = layer = 0
            for kind, c0, n in STAGES:
                if kind in ("da", "mix"):
                    groups = 2 if kind == "mix" else 4
                    lead = 2 if kind == "mix" else 0
                    g0 = c0 + lead
                    for k in range(lead):
                        project(c0 + k, slot_of(c0, k), app if k == 0 else None)
                    project(g0, slot_of(g0, 0), app if lead == 0 else None)
                    if c0 == 0:
                        bias_vectors()
                    project(g0 + 1, slot_of(g0, 1))
                    chunk_ready(g0 + 2)
                    project_tokens(slot_of(g0, 2), 0, 0, 2 * P, (0,))
                    pe.wait_ge(bank_free, RING + g0 + 1)
                    if c0 == 0:
                        pe.wait_ge(vec_sb, 3)
                    scores(s_half, 0, 1)
                    project_tokens(slot_of(g0, 2), 0, 0, 2 * P, (1,))
                    da = kind == "da"
                    maps = 1 if da else 2
                    cols = [[0], [P]] if da else [[0, 64], [P, P + 64]]

                    def head_statistic(d, slot):
                        pe.wait_ge(head_sq, d + 1)
                        pe.wait_ge(head_rstd, d * 2)
                        pe.matmul(tp[1][:, 0:S], ones, u_sb[:, 2 + slot, :], start=True, stop=True)\
                          .then_inc(head_stat, 1)

                    def beside(i, more, k, part):
                        at, slot = i * RING + (g0 + RING) + k, slot_of(g0, k)
                        if more:
                            if k < 2:
                                project_half(at, slot, part)
                            else:
                                if part == 0:
                                    chunk_ready(at)
                                project_tokens(slot, 0, 0, 2 * P, (part,))
                        elif da:
                            if part == 0:
                                pe.wait_ge(mix_lo, half + filled[k])
                            out_part(at, slot, part, 0, filled[k])
                        elif k == 0:
                            bank = pj[slot_of(g0, (0, 2)[part])]
                            if part == 0:
                                chunk_ready(at)
                                pe.wait_ge(pooled, POOL_STEPS)
                            else:
                                pe.wait_ge(bank_free, at + 3)
                            for g in (2 * part, 2 * part + 1):
                                done = product(bank[:, g % 2 * S:g % 2 * S + S], [w_tile(slot, g, P, 0)],
                                               [(act_hi[:, 16 + g, :], act_lo[:, 16 + g, :])])
                            if part:
                                done.then_inc(used, 1)
                        elif k == 1:
                            if part == 0:
                                chunk_ready(at)
                                pe.wait_ge(mix_lo, half + 2)
                            out_part(at, slot, part, 4, 6, start=part == 0)
                        else:
                            if part == 0:
                                pe.wait_ge(bank_free, at + 2)
                            out_part(at - 1, slot_of(g0, 1), part, 0, 4, start=False)

                    def group(i, more):
                        q, s, d = i * 2 + half, i * 2 + s_half, i * 2 + d_half
                        at = i * RING + (g0 + RING)
                        beside(i, more, 0, 0)
                        pe.wait_ge(bank_free, at + 2)
                        scores(s + 1, 2, 3)
                        beside(i, more, 0, 1)
                        transposes(s, 0, maps)
                        beside(i, more, 1, 0)
                        pe.wait_ge(bank_free, at + 3)
                        pe.wait_ge(probT_done, s + 1)
                        heads(q, 0, cols[0])
                        beside(i, more, 1, 1)
                        if da:
                            head_statistic(d, 0)
                        transposes(s + 1, 1, maps)
                        beside(i, more, 2, 0)
                        pe.wait_ge(probT_done, s + 2)
                        heads(q + 1, 1, cols[1])
                        if more:
                            pe.wait_ge(bank_free, at + (RING + 1))
                            scores(s + 2, 0, 1)
                        beside(i, more, 2, 1)
                        if da:
                            head_statistic(d + 1, 1)

                    filled = {0: 5, 1: 6, 2: 6} if da else {0: 6}
                    if groups > 2:
                        with pe.Fori(0, groups - 1) as i:
                            group(i, True)
                    else:
                        group(0, True)
                    group(groups - 1, False)
                    half += 2 * groups
                    s_half += 2 * groups
                    if da:
                        d_half += 2 * groups
                    app += 1
                elif kind == "sb":
                    def sb_scores(b, slot):
                        bank = (sc, tp)[slot]
                        for m in range(2):
                            q = proj[64 * m:64 * m + 64, 2 * slot, :]
                            k = proj[64 * m:64 * m + 64, 2 * slot + 1, :]
                            pe.matmul(bank[m][:, 0:S], k[:, 0:QB], q, start=True, stop=False,
                                      skip_group_check=True)
                            done = pe.matmul(bank[m][:, S:CAUSAL], k[:, QB:S], q[:, QB:S], start=False,
                                             stop=False, skip_group_check=True)
                        done.then_inc(scores_done, 1)

                    def cumulate(b, slot):
                        pe.wait_ge(sp_masked, (b + slot) * 2 + 2)
                        bank = (sc, tp)[slot]
                        for m in range(2):
                            sp_ = prob[:, slot, m, :]
                            pe.matmul(bank[m][:, 0:S], neg_tri, sp_[:, 0:S], start=False, stop=False,
                                      skip_group_check=True)
                            pe.matmul(bank[m][:, QB:S], neg_ones, sp_[:, S:CAUSAL], start=False, stop=False,
                                      skip_group_check=True)
                            done = pe.matmul(bank[m][:, S:CAUSAL], neg_tri, sp_[:, S:CAUSAL], start=False,
                                             stop=True, skip_group_check=True)
                        done.then_inc(cum_done, 1)

                    filled = {0: 6, 1: 6, 2: 6}

                    def out_parts(at, k):
                        pe.wait_ge(mix_lo, half + filled[k])
                        for part in range(2):
                            out_part(at + k, slot_of(c0, k), part, 0, filled[k])

                    def group(i, more):
                        b, q = i * 2, i * 2 + half
                        at = i * RING + (c0 + RING)
                        if more:
                            project(at, slot_of(c0, 0))
                        else:
                            out_parts(at, 0)
                        cumulate(b, 0)
                        cumulate(b, 1)
                        if more:
                            project(at + 1, slot_of(c0, 1))
                        else:
                            out_parts(at, 1)
                        pe.wait_ge(bank_free, at + 3)
                        pe.wait_ge(a_masked, b * 2 + 2)
                        heads(q, 0, [0, 64])
                        if more:
                            project_v(at + 2, slot_of(c0, 2))
                        else:
                            out_parts(at, 2)
                        pe.wait_ge(a_masked, b * 2 + 4)
                        heads(q + 1, 1, [P, P + 64])
                        if more:
                            pe.wait_ge(bank_free, at + (RING + 2))
                            sb_scores(b + 2, 0)
                            sb_scores(b + 2, 1)

                    project(c0, slot_of(c0, 0), app)
                    project(c0 + 1, slot_of(c0, 1))
                    project_v(c0 + 2, slot_of(c0, 2))
                    pe.wait_ge(bank_free, RING + c0 + 2)
                    sb_scores(0, 0)
                    sb_scores(0, 1)
                    with pe.Fori(0, 3) as i:
                        group(i, True)
                    group(3, False)
                    half += 8
                    app += 1
                elif kind == "sw":
                    def v_at(j):
                        return P * (j // 4)

                    def kv(c, part):
                        slot = c % RING
                        if part == 0:
                            chunk_ready(c)
                            outputs(slot, 0, pj[slot][:, 0:S])
                        else:
                            project_tokens(slot, S, P, P)

                    slot0 = slot_of(c0, 0)
                    chunk_ready(c0)
                    first_outputs(app, [(pj[slot0][:, 0:S], lambda k: (w_tile(slot0, k, 2 * P, 0), h_tile(k), False))]
                                  + [(pj[slot0][:, S + b * P:S + b * P + P],
                                      lambda k, b=b: (w_tile(slot0, k, 2 * P, P), h_tile(k, b * P, b * P + P), True))
                                     for b in range(2)]).then_inc(used, 1)
                    project(c0 + 1, slot_of(c0, 1))
                    project_half(c0 + 2, slot_of(c0, 2), 0)
                    pe.wait_ge(bank_free, RING + c0 + 2)
                    scores(s_half, 0, 4)
                    project_half(c0 + 2, slot_of(c0, 2), 1)
                    scores(s_half + 1, 1, 4)
                    outs = {3: (0, 0, 3), 4: (1, 0, 4), 5: (2, 0, 5), 6: (0, 3, 6), 7: (1, 4, 6)}
                    filled = {0: 6, 1: 6, 2: 5}

                    def beside(j, part):
                        if j == 0:
                            kv(c0 + 3, part)
                        elif j < 3:
                            project_half(c0 + 3 + j, slot_of(c0, j), part)
                        else:
                            k, a, b = outs[j]
                            pe.wait_ge(mix_lo, half + b)
                            out_part(c0 + n + k, slot_of(c0, k), part, a, b)

                    for j in range(8):
                        q, s = half + j, s_half + j
                        transposes(s, j % 2, 2)
                        if j < 3:
                            beside(j, 0)
                        if j < 6:
                            pe.wait_ge(bank_free, RING + c0 + (3, 3, 5, 5, 6, 6)[j])
                            scores(s + 2, (j + 2) % 4, 4 if j < 2 else None)
                        if j >= 3:
                            beside(j, 0)
                        pe.wait_ge(probT_done, s + 1)
                        heads(q, j % 2, [v_at(j), v_at(j) + 64])
                        beside(j, 1)
                    half += 8
                    s_half += 8
                    app += 1
                elif kind == "wo":
                    for k in range(4):
                        slot = slot_of(c0, k)
                        a = filled.get(k, 0)
                        if a == 0:
                            chunk_ready(c0 + k)
                        if k == 0:
                            pe.wait_ge(mix_lo, half)
                            if layer == 4:
                                pe.wait_ge(bank_free, RING + c0)
                        if k < 3:
                            for t in range(2):
                                out_part(c0 + k, slot, t, a, DT)
                        else:
                            out_part(c0 + k, slot, 0, 0, DT).then_inc(tile6_done, 1)
                            out_part(c0 + k, slot, 1, 0, DT, val_bank[slot][:, 0:S])
                    statistic(f"wo{layer}")
                    if layer == 4:
                        statistic("res_a")
                elif kind == "up":
                    def up(c, slot):
                        chunk_ready(c)
                        outputs(slot, 0, pj[slot][:, 0:S])
                        outputs(slot, 1, val_bank[slot][:, 0:S]).then_inc(used, 1)

                    slot0 = slot_of(c0, 0)
                    pair(c0, slot0, (pj[slot0][:, 0:S], val_bank[slot0][:, 0:S]), app, shared=False)
                    with pe.Fori(0, (n - 1) // RING) as i:
                        for k in range(RING):
                            up(i * RING + (c0 + 1 + k), slot_of(c0, 1 + k))
                    app += 1
                elif kind == "down":
                    def down(c, slot, a=0, b=FT):
                        if a == 0:
                            chunk_ready(c)
                        done = product(pj[slot][:, 0:S], [w_tile(slot, k, P, 0) for k in range(a, b)],
                                       [(act_hi[:, k, :], act_lo[:, k, :]) for k in range(a, b)],
                                       start=a == 0, stop=b == FT)
                        if b == FT:
                            done.then_inc(used, 1)

                    early = FT - 3
                    pe.wait_ge(act_free, RING + ffn * FT + early)
                    for k in range(2):
                        down(c0 + k, slot_of(c0, k), 0, early)
                    pe.wait_ge(act_free, RING + ffn * FT + FT)
                    for k in range(2):
                        down(c0 + k, slot_of(c0, k), early, FT)
                    with pe.Fori(0, 2) as i:
                        for k in range(RING):
                            down(i * RING + (c0 + 2 + k), slot_of(c0, 2 + k))
                    statistic(f"down{layer}")
                    if layer == 3:
                        statistic("final")
                    ffn += 1
                    layer += 1
                else:
                    def embedding(k):
                        slot = slot_of(c0, k)
                        chunk_ready(c0 + k)
                        for t in range(2):
                            product(val_bank[k % 3][:, t * S:t * S + S],
                                    [w_tile(slot, DT + f, 2 * P, t * P) for f in range(2)],
                                    [(act_hi[:, f, :], act_lo[:, f, :]) for f in range(2)])

                    pe.wait_ge(p_lo, 1)
                    embedding(0)
                    embedding(1)
                    slot0 = slot_of(c0, 0)
                    for k in range(n):
                        slot = slot_of(c0, k)
                        if k > 1:
                            embedding(k)
                        if k == 0:
                            first_outputs(app, [(pj[slot][:, t * S:t * S + S],
                                                 lambda k_, t=t: (w_tile(slot0, k_, 2 * P, t * P), h_tile(k_), False))
                                                for t in range(2)]).then_inc(used, 1)
                            continue
                        outputs(slot, 0, pj[slot][:, 0:S])
                        outputs(slot, 1, pj[slot][:, S:2 * S]).then_inc(used, 1)


def _rows(w):
    return w.reshape(-1, P, w.shape[-1]).transpose(1, 0, 2)


def _chunk(*columns):
    return _rows(np.concatenate(columns, axis=1)).reshape(P, -1)


def _vector(v):
    return v.reshape(-1, P).T


def _heads(w, heads):
    return np.concatenate([w[:, 64 * h:64 * h + 64] for h in heads], axis=1)


def _buckets():
    dist = np.arange(NVEC) - 127
    d = np.maximum(dist, 0)
    large = 16 + (np.log(np.maximum(d, 1).astype(np.float32) / np.float32(16))
                  / np.float32(np.log(128 / 16)) * np.float32(16)).astype(np.int32)
    bucket = np.where(d < 16, d, np.minimum(large, 31))
    return dist, np.where(dist < 0, 32, bucket)


def kernel(**inputs):
    import concourse.bacc as bacc
    from concourse.bass_utils import run_bass_kernel_spmd as run

    a = {k: np.asarray(v) for k, v in inputs.items()}
    FF = a["ffn_w_down"].shape[1]

    std, down = [], []

    def grouped(w, first, groups, k_at, v_at):
        for i in range(groups):
            for t in (2 * i, 2 * i + 1):
                std.append(_chunk(w[:, first + P * t:first + P * t + P], w[:, k_at + P * t:k_at + P * t + P]))
            std.append(_chunk(w[:, v_at + 2 * P * i:v_at + 2 * P * i + 2 * P]))

    def pairs(w):
        for k in range(4):
            std.append(_chunk(w[:, 2 * P * k:2 * P * k + 2 * P]))

    def ffn(up, dn, width):
        pad = FT * P - width
        gate, val = (np.pad(up[:, g * width:(g + 1) * width], ((0, 0), (0, pad))) for g in range(2))
        for j in range(FT):
            std.append(_chunk(gate[:, P * j:P * j + P], val[:, P * j:P * j + P]))
        dn = np.pad(dn, ((0, pad), (0, 0)))
        for f in range(DT):
            down.append(_chunk(dn[:, P * f:P * f + P]))

    sw_tiles = [(8 * t + j, 8 * t + 4 + j) for t in range(2) for j in range(4)]
    for layer in range(4):
        w_o = a["w_o"][layer]
        if layer % 3 == 0:
            grouped(a["da_w_qkv"][layer // 3], 0, 4, D, 2 * D)
        elif layer == 1:
            grouped(a["sb_w_qkv"][0], 0, 4, D, 2 * D)
        else:
            w = a["sw_w_qkv"][0]
            for t in range(2):
                std.append(_chunk(w[:, D + P * t:D + P * t + P], w[:, D + 256 + P * t:D + 256 + P * t + P]))
                for j in (0, 2):
                    std.append(_chunk(*[_heads(w, sw_tiles[4 * t + j + e]) for e in range(2)]))
            w_o = np.concatenate([w_o[64 * h:64 * h + 64] for pair in sw_tiles for h in pair])
        pairs(w_o)
        ffn(a["ffn_w_up"][layer], a["ffn_w_down"][layer], FF)
    w_in = a["w_in_2"][0]
    for k in range(2):
        std.append(_chunk(w_in[:, 2 * P * k:2 * P * k + 2 * P]))
    grouped(w_in, 512, 2, 1024, 1536)
    std.append(np.pad(a["w_pool_2"][0].transpose(1, 0, 2).reshape(P, 4 * P), ((0, 0), (0, STD - 4 * P))))
    pairs(a["w_out_2"][0])
    ffn(a["w_up_2"][0], a["w_down_2"][0], a["w_down_2"].shape[1])
    gate = [np.concatenate([_chunk(a[w][0][:, 2 * P * k:2 * P * k + 2 * P]) for w in ("w_ple_gate_2", "w_ple_2")],
                           axis=1) for k in range(4)]

    par = np.zeros((P, NPAR), np.float32)

    def put(name, value, k=0):
        par[:, PARAM[name] + k:PARAM[name] + k + value.shape[1]] = value

    for layer in range(4):
        put("attn_norm", _vector(a["attn_norm"][layer]), DT * layer)
        put("ffn_norm", _vector(a["ffn_norm"][layer]), DT * layer)
        taps = np.concatenate([a["ffn_conv_w"][layer], a["ffn_conv_b"][layer][None]])
        taps = np.pad(taps.reshape(4, 2, FF), ((0, 0), (0, 0), (0, FT * P - FF)))
        put("conv", taps.reshape(4, 2, FT, P).transpose(3, 2, 1, 0).reshape(P, -1), FT * 8 * layer)
    for name, source in (("mix_pre", "g_mix_pre_2"), ("mix_post", "g_mix_post_2"),
                         ("ffn_pre", "g_ffn_pre_2"), ("ffn_post", "g_ffn_post_2")):
        put(name, _vector(a[source][0]))
    put("final_norm", _vector(a["final_norm"]))
    taps = np.concatenate([a["conv_w_2"][0], a["conv_b_2"][0][None]])
    put("conv2", taps.reshape(4, FT, P).transpose(2, 1, 0).reshape(P, -1))
    put("subln", a["da_subln"].T)
    sinks = a["sw_sinks"][0][np.array(sw_tiles)]
    put("sinks", np.broadcast_to(np.repeat(sinks, 2, axis=1).reshape(1, -1), (P, 32)))
    put("pool_scale", _vector(a["pool_scale_2"][0]))
    counts = [1.0 / min(t + 1, w) for w in WINDOWS for t in range(16)]
    put("inv_count", np.broadcast_to(np.array(counts, np.float32), (P, 64)))

    rows = np.arange(P)
    consts = np.concatenate([np.eye(P), np.ones((P, P)), -(rows[:, None] >= rows[None, :]).astype(np.float32),
                             -np.ones((P, P))], axis=1).astype(np.float32)
    dist, bucket = _buckets()
    onehot = (bucket[None, :] == np.arange(33)[:, None]).astype(np.float32)
    windowed = np.where(dist >= 128, 32, bucket)
    onehot_w = (windowed[None, :] == np.arange(33)[:, None]).astype(np.float32)
    rel, rel2 = a["rel_bias"], a["rel_bias_2"]
    tables = np.full((33, 48), NEG, np.float32)
    tables[0:32, 0:16] = rel
    tables[0:32, 16:32] = rel[:, np.array(sw_tiles).reshape(-1)]
    tables[0:32, 32:40] = rel2
    tables[:, 40:48] = 0.0

    arrays = {
        "xT": _rows(a["x"][0].T), "w_std": np.stack(std), "w_down": np.stack(down), "w_gate": np.stack(gate),
        "params": par, "consts": consts, "lam": np.broadcast_to(a["da_lambda"].reshape(1, 2, 256), (P, 2, 256)),
        "onehot": np.stack([onehot, onehot_w]), "tables": tables, "pT": _rows(a["p_2"][0, 0].T),
    }
    arrays = {k: np.ascontiguousarray(v) for k, v in arrays.items()}
    nc = bacc.Bacc("TRN2", target_bir_lowering=False, num_devices=1)
    args = [nc.dram_tensor(k, v.shape, mybir.dt.from_np(v.dtype), kind="ExternalInput").ap()
            for k, v in arrays.items()]
    out = nc.dram_tensor("out", (P, DT, S), F32, kind="ExternalOutput").ap()
    build(nc, *args, out)
    got = run(nc, [arrays], core_ids=[0]).results[0]["out"]
    return np.ascontiguousarray(got.transpose(1, 0, 2).reshape(D, S).T)[None]
```
